# Optimizing a Trainium2 kernel written in Bass

```python
import math
import jax, jax.numpy as jnp
from jax import lax
import numpy as np

D_MODEL = 2048
BATCH = 1
SEQ = 512
DEPTH = 1

HEAD_DIM = 128
A_HEADS = 8
A_KV_HEADS = 2
A_GROUP = A_HEADS // A_KV_HEADS
A_WIDTH = A_HEADS * HEAD_DIM
A_KV_WIDTH = A_KV_HEADS * HEAD_DIM
WINDOW = 128
A_BLOCK = 128
NUM_BUCKETS = 32
MAX_DISTANCE = 128
B_HEADS = 8
B_WIDTH = B_HEADS * HEAD_DIM
GRID_W = 64
NB_ROWS = 8
NB_COLS = 16
IN_COLS = A_WIDTH + 2 * A_KV_WIDTH + 3 * B_WIDTH + 2 * D_MODEL
N_GROUPS = 4
EXPERTS_PER_GROUP = 8
N_EXPERTS = N_GROUPS * EXPERTS_PER_GROUP
TOP_K = 2
D_EXPERT = 512
MOE_BLOCK = 128
EPS = 1e-6
NEG_INF = -1e30

kernel_name = "hybrid_window_gqa_natten_hier_moe"

def rms_norm(x, g):
    xf = x.astype(jnp.float32)
    y = xf * lax.rsqrt(jnp.mean(xf * xf, axis=-1, keepdims=True) + EPS)
    return (y * g.astype(jnp.float32)).astype(x.dtype)

def t5_bucket(rel):
    nb = NUM_BUCKETS // 2
    ret = jnp.where(rel > 0, nb, 0)
    n = jnp.abs(rel)
    max_exact = nb // 2
    nf = jnp.maximum(n, 1).astype(jnp.float32)
    large = max_exact + (jnp.log(nf / max_exact) / math.log(MAX_DISTANCE / max_exact)
                         * (nb - max_exact)).astype(jnp.int32)
    large = jnp.minimum(large, nb - 1)
    return ret + jnp.where(n < max_exact, n, large)

def window_gqa(q, k, v, g_q, g_k, rel_table, sink):
    B, S = q.shape[0], q.shape[1]
    nb = S // A_BLOCK
    q = rms_norm(q.reshape(B, S, A_HEADS, HEAD_DIM), g_q)
    k = rms_norm(k.reshape(B, S, A_KV_HEADS, HEAD_DIM), g_k)
    v = v.reshape(B, S, A_KV_HEADS, HEAD_DIM)
    qb = q.reshape(B, nb, A_BLOCK, A_KV_HEADS, A_GROUP, HEAD_DIM)

    def band(t):
        tp = jnp.pad(t, ((0, 0), (WINDOW, WINDOW), (0, 0), (0, 0)))
        tp = tp.reshape(B, nb + 2, A_BLOCK, A_KV_HEADS, HEAD_DIM)
        return jnp.concatenate([tp[:, :-2], tp[:, 1:-1], tp[:, 2:]], axis=2)

    kw, vw = band(k), band(v)
    s = jnp.einsum('bnqhgd,bnkhd->bnhgqk', qb, kw).astype(jnp.float32) * (HEAD_DIM ** -0.5)
    q_loc = jnp.arange(A_BLOCK)
    k_loc = jnp.arange(3 * A_BLOCK) - WINDOW
    rel = k_loc[None, :] - q_loc[:, None]
    bias = rel_table[t5_bucket(rel)].astype(jnp.float32)
    bias = jnp.transpose(bias, (2, 0, 1)).reshape(A_KV_HEADS, A_GROUP, A_BLOCK, 3 * A_BLOCK)
    k_pos = jnp.arange(nb)[:, None] * A_BLOCK + k_loc[None, :]
    valid = (jnp.abs(rel) <= WINDOW)[None] & ((k_pos >= 0) & (k_pos < S))[:, None, :]
    s = jnp.where(valid[None, :, None, None], s + bias, NEG_INF)
    sink_col = jnp.broadcast_to(sink.astype(jnp.float32).reshape(A_KV_HEADS, A_GROUP, 1, 1),
                                s.shape[:-1] + (1,))
    p = jax.nn.softmax(jnp.concatenate([s, sink_col], axis=-1), axis=-1)[..., :-1]
    o = jnp.einsum('bnhgqk,bnkhd->bnqhgd', p.astype(v.dtype), vw)
    return o.reshape(B, S, A_WIDTH)

def neighbourhood_attention(q, k, v, g_q, g_k, rpb):
    B, S = q.shape[0], q.shape[1]
    R = S // GRID_W
    kh = min(NB_ROWS, R)
    q = rms_norm(q.reshape(B, R, GRID_W, B_HEADS, HEAD_DIM), g_q)
    k = rms_norm(k.reshape(B, R, GRID_W, B_HEADS, HEAD_DIM), g_k)
    v = v.reshape(B, R, GRID_W, B_HEADS, HEAD_DIM)
    cols = jnp.arange(GRID_W)
    col_idx = jnp.clip(cols - NB_COLS // 2, 0, GRID_W - NB_COLS)[:, None] + jnp.arange(NB_COLS)[None, :]
    dc = col_idx - cols[:, None] + (NB_COLS - 1)
    scale = HEAD_DIM ** -0.5

    def row(r):
        rs = jnp.clip(r - kh // 2, 0, R - kh)
        q_r = lax.dynamic_index_in_dim(q, r, axis=1, keepdims=False)
        k_nb = lax.dynamic_slice_in_dim(k, rs, kh, axis=1)[:, :, col_idx]
        v_nb = lax.dynamic_slice_in_dim(v, rs, kh, axis=1)[:, :, col_idx]
        s = jnp.einsum('bqhd,brqjhd->bhqrj', q_r, k_nb).astype(jnp.float32) * scale
        dr = rs + jnp.arange(kh) - r + (NB_ROWS - 1)
        bias = rpb[:, dr[None, :, None], dc[:, None, :]].astype(jnp.float32)
        s = s + bias[None]
        p = jax.nn.softmax(s.reshape(B, B_HEADS, GRID_W, kh * NB_COLS), axis=-1).reshape(s.shape)
        return jnp.einsum('bhqrj,brqjhd->bqhd', p.astype(v.dtype), v_nb)

    o = lax.map(row, jnp.arange(R))
    return jnp.moveaxis(o, 0, 1).reshape(B, S, B_WIDTH)

def mixer_sublayer(x, norm_g, w_in, q_norm_a, k_norm_a, sink_a, q_norm_b, k_norm_b, rpb_b,
                   w_up_a, w_up_b, w_out, rel_table):
    xn = rms_norm(x, norm_g)
    proj = xn @ w_in
    cuts = np.cumsum([A_WIDTH, A_KV_WIDTH, A_KV_WIDTH, B_WIDTH, B_WIDTH, B_WIDTH, D_MODEL])
    qa, ka, va, qb, kb, vb, ga, gb = jnp.split(proj, [int(c) for c in cuts], axis=-1)
    oa = window_gqa(qa, ka, va, q_norm_a, k_norm_a, rel_table, sink_a)
    ob = neighbourhood_attention(qb, kb, vb, q_norm_b, k_norm_b, rpb_b)
    merged = jax.nn.sigmoid(ga) * (oa @ w_up_a) + jax.nn.sigmoid(gb) * (ob @ w_up_b)
    return x + merged @ w_out

def hier_moe(xn, w_rg, b_rg, w_re, b_re, w_gate, w_up, w_down):
    T, D = xn.shape
    g_logits = (xn @ w_rg).astype(jnp.float32) + b_rg.astype(jnp.float32)
    g_idx = jnp.argmax(g_logits, axis=-1)
    p_g = jnp.take_along_axis(jax.nn.softmax(g_logits, axis=-1), g_idx[:, None], axis=-1)
    e_all = ((xn @ w_re).astype(jnp.float32) + b_re.astype(jnp.float32)).reshape(T, N_GROUPS, EXPERTS_PER_GROUP)
    e_logits = jnp.take_along_axis(e_all, g_idx[:, None, None], axis=1)[:, 0]
    top_v, top_e = lax.top_k(e_logits, TOP_K)
    weight = p_g * jax.nn.softmax(top_v, axis=-1)
    expert_id = g_idx[:, None] * EXPERTS_PER_GROUP + top_e

    A = T * TOP_K
    flat_e = expert_id.reshape(A).astype(jnp.int32)
    flat_tok = jnp.repeat(jnp.arange(T, dtype=jnp.int32), TOP_K)
    flat_w = weight.reshape(A)
    order = jnp.argsort(flat_e)
    se, st, sw = flat_e[order], flat_tok[order], flat_w[order]
    counts = jnp.bincount(flat_e, length=N_EXPERTS).astype(jnp.int32)
    padded = ((counts + MOE_BLOCK - 1) // MOE_BLOCK) * MOE_BLOCK
    end_pad = jnp.cumsum(padded)
    start_pad = end_pad - padded
    start_orig = jnp.cumsum(counts) - counts
    dest = start_pad[se] + (jnp.arange(A, dtype=jnp.int32) - start_orig[se])
    P = A + N_EXPERTS * MOE_BLOCK
    NB = P // MOE_BLOCK
    buf_tok = jnp.full((P,), T, jnp.int32).at[dest].set(st)
    buf_w = jnp.zeros((P,), jnp.float32).at[dest].set(sw)
    blk_e = jnp.minimum(jnp.searchsorted(end_pad, jnp.arange(NB, dtype=jnp.int32) * MOE_BLOCK, side='right'),
                        N_EXPERTS - 1)
    x_pad = jnp.concatenate([xn, jnp.zeros((1, D), xn.dtype)], axis=0)

    def expert_block(args):
        e, tok, w = args
        rows = x_pad[tok]
        h = jax.nn.silu(rows @ w_gate[e]) * (rows @ w_up[e])
        return (h @ w_down[e]) * w[:, None].astype(rows.dtype)

    yb = lax.map(expert_block, (blk_e, buf_tok.reshape(NB, MOE_BLOCK), buf_w.reshape(NB, MOE_BLOCK)))
    y = jnp.zeros((T + 1, D), xn.dtype).at[buf_tok].add(yb.reshape(P, D))
    return y[:T]

def setup_inputs(seed: int = 0) -> dict:
    key = jax.random.key(seed)
    ks = jax.random.split(key, 21)
    f32 = jnp.float32
    L = DEPTH

    def nrm(k, shape, scale):
        return jax.random.normal(k, shape, f32) * scale

    return {
        "x": nrm(ks[0], (BATCH, SEQ, D_MODEL), 1.0),
        "norm1_g": 1.0 + nrm(ks[1], (L, D_MODEL), 0.02),
        "w_in": nrm(ks[2], (L, D_MODEL, IN_COLS), D_MODEL ** -0.5),
        "q_norm_a": 1.0 + nrm(ks[3], (L, HEAD_DIM), 0.02),
        "k_norm_a": 1.0 + nrm(ks[4], (L, HEAD_DIM), 0.02),
        "sink_a": nrm(ks[5], (L, A_HEADS), 0.5),
        "q_norm_b": 1.0 + nrm(ks[6], (L, HEAD_DIM), 0.02),
        "k_norm_b": 1.0 + nrm(ks[7], (L, HEAD_DIM), 0.02),
        "rpb_b": nrm(ks[8], (L, B_HEADS, 2 * NB_ROWS - 1, 2 * NB_COLS - 1), 0.1),
        "w_up_a": nrm(ks[9], (L, A_WIDTH, D_MODEL), A_WIDTH ** -0.5),
        "w_up_b": nrm(ks[10], (L, B_WIDTH, D_MODEL), B_WIDTH ** -0.5),
        "w_out": nrm(ks[11], (L, D_MODEL, D_MODEL), D_MODEL ** -0.5),
        "rel_bias_table": nrm(ks[12], (NUM_BUCKETS, A_HEADS), 0.1),
        "norm2_g": 1.0 + nrm(ks[13], (L, D_MODEL), 0.02),
        "w_router_group": nrm(ks[14], (L, D_MODEL, N_GROUPS), D_MODEL ** -0.5),
        "b_router_group": nrm(ks[15], (L, N_GROUPS), 0.01),
        "w_router_expert": nrm(ks[16], (L, D_MODEL, N_EXPERTS), D_MODEL ** -0.5),
        "b_router_expert": nrm(ks[17], (L, N_EXPERTS), 0.01),
        "w_gate": nrm(ks[18], (L, N_EXPERTS, D_MODEL, D_EXPERT), D_MODEL ** -0.5),
        "w_up": nrm(ks[19], (L, N_EXPERTS, D_MODEL, D_EXPERT), D_MODEL ** -0.5),
        "w_down": nrm(ks[20], (L, N_EXPERTS, D_EXPERT, D_MODEL), D_EXPERT ** -0.5),
    }

def reference(x, norm1_g, w_in, q_norm_a, k_norm_a, sink_a, q_norm_b, k_norm_b, rpb_b,
              w_up_a, w_up_b, w_out, rel_bias_table, norm2_g, w_router_group, b_router_group,
              w_router_expert, b_router_expert, w_gate, w_up, w_down):
    B, S, D = x.shape
    h = x
    for l in range(DEPTH):
        h = mixer_sublayer(h, norm1_g[l], w_in[l], q_norm_a[l], k_norm_a[l], sink_a[l],
                           q_norm_b[l], k_norm_b[l], rpb_b[l], w_up_a[l], w_up_b[l], w_out[l],
                           rel_bias_table)
        hn = rms_norm(h, norm2_g[l]).reshape(B * S, D)
        h = h + hier_moe(hn, w_router_group[l], b_router_group[l], w_router_expert[l],
                         b_router_expert[l], w_gate[l], w_up[l], w_down[l]).reshape(B, S, D)
    return h


_drawn_inputs = setup_inputs


def setup_inputs(seed=0):
    import zlib

    import numpy as np

    out = dict(_drawn_inputs(seed))
    spreads = {}
    factors = {'norm1_g': 5.179,
     'q_norm_a': 8.0,
     'k_norm_a': 8.0,
     'sink_a': 8.0,
     'q_norm_b': 8.0,
     'k_norm_b': 5.21,
     'rpb_b': 2.671,
     'rel_bias_table': 3.575,
     'b_router_group': 64.0,
     'b_router_expert': 28.504,
     'norm2_g': 8.0}
    for name, (base, spread) in spreads.items():
        noise = np.random.default_rng([zlib.crc32(name.encode()), seed]).standard_normal(out[name].shape)
        drawn = base * np.exp(spread * noise) if base else spread * noise
        out[name] = __import__('jax').numpy.asarray(drawn.astype(out[name].dtype))
    for name, factor in factors.items():
        out[name] = (out[name] * factor).astype(out[name].dtype)
    return out
```

```python
from contextlib import ExitStack

import numpy as np
import concourse.bass as bass
from concourse import mybir

F32 = mybir.dt.float32
F32R = mybir.dt.float32r
U32 = mybir.dt.uint32
I32 = mybir.dt.int32
ALU = mybir.AluOpType
ACT = mybir.ActivationFunctionType
AX = mybir.AxisListType.X
ds = bass.ds

P = 128
D = 2048
S = 512
KT = D // P
NT = S // P
HD = 128
A_HEADS, A_KV, A_GROUP = 8, 2, 4
B_HEADS = 8
HEADS = A_HEADS + B_HEADS
BUCKETS, WINDOW, MAXDIST = 32, 128, 128
GRID_W, ROWS = 64, S // 64
NB_ROWS, NB_COLS = 8, 16
QC = GRID_W // NT
KC = 2 * QC
B_START = [min(max(QC * b - NB_COLS // 2, 0), GRID_W - KC) for b in range(NT)]
B_KIND = [(QC * b - B_START[b]) // 8 for b in range(NT)]
A_WIDTH, A_KVW, B_WIDTH = A_HEADS * HD, A_KV * HD, B_HEADS * HD
COL_QA = 0
COL_KA = A_WIDTH
COL_VA = COL_KA + A_KVW
COL_QB = COL_VA + A_KVW
COL_KB = COL_QB + B_WIDTH
COL_VB = COL_KB + B_WIDTH
COL_GA = COL_VB + B_WIDTH
COL_GB = COL_GA + D
GROUPS, PER_GROUP, EXPERTS, F = 4, 8, 32, 512
LOG = GROUPS + EXPERTS
EPS = 1e-6
NEG = -1e30
SLOTS = 64
MORE = S // SLOTS - 1
XTRA = 2 * S // SLOTS
ITEMS = EXPERTS + XTRA + 1
RPB_W = 2 * NB_COLS - 1 + 2 * NB_COLS
RAW, SPLIT = 3, 2
CH_A = 0
CH_B = CH_A + 2 * (A_KV * 2 + A_HEADS)
CH_M = CH_B + 6 * B_HEADS
CH_O = CH_M + 6 * KT
CH_END = CH_O + NT * 8


def a_keys(b):
    return (P if b == 0 else 0), (2 * P if b == NT - 1 else 3 * P)


class Chain:

    def __init__(self, eng, sem):
        self.eng, self.sem, self.base, self.n = eng, sem, 0, 0

    def link(self, ins):
        self.n += 1
        ins.then_inc(self.sem, 1)
        return ins

    def wait(self, back=0):
        self.eng.wait_ge(self.sem, self.base + (self.n - back))

    def do(self, ins):
        self.link(ins)
        self.wait()

    def loop(self, i, first, per):
        self.start, self.per, self.rounds = self.base + self.n, per, None
        self.base, self.n = (i - first) * per + self.start, 0

    def done(self, rounds):
        assert self.n == self.per, (self.n, self.per)
        self.base, self.n = 0, self.start + rounds * self.per


def bc(ap, n):
    return bass.AP(ap.tensor, ap.offset, [list(x) for x in ap.ap] + [[0, n]])


def rep(ap, n):
    a = [list(x) for x in ap.ap]
    return bass.AP(ap.tensor, ap.offset, a[:1] + [[0, n]] + a[1:])


def build(nc, x, norm1_g, w_in, q_norm_a, k_norm_a, sink_a, q_norm_b, k_norm_b, rpb_pad, w_up_a, w_up_b,
          w_out, rel_bias_table, norm2_g, w_router_group, b_router_group, w_router_expert,
          b_router_expert, w_gate, w_up, w_down, c_mats, c_onehot, c_maska, c_maskb, c_ramp, c_entry,
          c_tokens, tvec_d, h_d, wide_d, bias_d, out):
    ctx = ExitStack()
    with ctx:
        at = [0]

        def sb(name, shape, dt, offset):
            size = 4 * int(np.prod(shape[1:]))
            at[0] = offset + size
            return nc.alloc_sbuf_tensor_at(name, shape, dt, offset=offset)

        def sem(name):
            return ctx.enter_context(nc.semaphore(name))

        K = 1024
        base = -(-nc.sbuf_base // 32) * 32
        R0, R1, R2, R3, R4 = (base + n * K for n in (0, 64, 128, 160, 198))
        x_hi = sb("x_hi", [P, KT, S], F32R, R0)
        x_lo = sb("x_lo", [P, KT, S], F32R, R0 + 32 * K)
        m_hi = sb("m_hi", [P, KT, S], F32R, R0)
        m_lo = sb("m_lo", [P, KT, S], F32R, R0 + 32 * K)
        wd_s = sb("wd_s", [P, 4, D], F32, R0)
        xg = sb("xg", [SLOTS, D], F32, R0 + 32 * K)
        xT = sb("xT", [P, KT, SLOTS], F32, R0 + 40 * K)
        y_hi = sb("y_hi", [P, D // 2], F32R, R0 + 44 * K)
        y_lo = sb("y_lo", [P, D // 2], F32R, R0 + 48 * K)
        sg = sb("sg", [P, F // 2], F32, R0 + 52 * K)
        t1 = sb("t1", [P, F // 2], F32, R0 + 53 * K)
        hs = sb("hs", [P, F // 2], F32, R0 + 54 * K)
        hT = sb("hT", [P, 2, P], F32, R0 + 55 * K)
        place = sb("place", [P, S], F32R, R0 + 56 * K)
        token = sb("token", [P, S], F32, R0 + 58 * K)
        tab = sb("tab", [P, 3, ITEMS], F32, R0 + 60 * K)
        idx_x = sb("idx_x", [SLOTS, ITEMS], U32, R0 + 61 * K)
        cur_x = sb("cur_x", [SLOTS, 1], U32, R0 + 61 * K + 256)
        cur = sb("cur", [P, 2], F32, R0 + 61 * K + 288)
        xt = sb("xt", [P, NT, D], F32, R1)
        o_hi = sb("o_hi", [P, HEADS, S], F32R, R1)
        o_lo = sb("o_lo", [P, HEADS, S], F32R, R1 + 32 * K)
        h = sb("h", [P, NT, D], F32, R1)
        wg_s = sb("wg_s", [P, KT, F], F32, R1 + 32 * K)
        w_raw = sb("w_raw", [P, RAW, 8 * P], F32, R2)
        bias = sb("bias", [P, 3, 2 * P], F32, R2 + 12 * K)
        w_hi = sb("w_hi", [P, SPLIT, 8 * P], F32R, R2 + 16 * K)
        w_lo = sb("w_lo", [P, SPLIT, 8 * P], F32R, R2 + 24 * K)
        gb = sb("gb", [P, D], F32, R3)
        junk = sb("junk", [P, D], F32, R3 + 8 * K)
        v_hi = sb("v_hi", [P, 8, P], F32R, R3)
        v_lo = sb("v_lo", [P, 8, P], F32R, R3 + 4 * K)
        q_hi = sb("q_hi", [P, S], F32R, R3 + 8 * K)
        q_lo = sb("q_lo", [P, S], F32R, R3 + 10 * K)
        prob = sb("prob", [P, 4, 3 * P], F32, R3 + 12 * K)
        rk = sb("rk", [P, S], F32, R3 + 12 * K)
        pt_hi = sb("pt_hi", [P, 4, 3 * P], F32R, R3 + 18 * K)
        pt_lo = sb("pt_lo", [P, 4, 3 * P], F32R, R3 + 24 * K)
        kn = sb("kn", [P, S], F32, R3 + 30 * K)
        sq = sb("sq", [P, S], F32, R3 + 32 * K)
        vt = sb("vt", [P, S], F32, R3 + 32 * K)
        k_hi = sb("k_hi", [P, S], F32R, R3 + 34 * K)
        k_lo = sb("k_lo", [P, S], F32R, R3 + 36 * K)
        m_raw = sb("m_raw", [P, KT, S], F32, R3)
        sig_a = sb("sig_a", [P, S], F32, R3 + 32 * K)
        t_a = sb("t_a", [P, S], F32, R3 + 34 * K)
        sig_b = sb("sig_b", [P, S], F32, R3 + 36 * K)
        wu_s = sb("wu_s", [P, KT, F], F32, R3)
        x_res = sb("x_res", [P, 3, S], F32, R3 + 32 * K)
        x_last = sb("x_last", [P, S], F32, R2 + 12 * K)
        o4 = R4
        mats = sb("mats", [P, 3, P], F32, o4)
        mask_b = sb("mask_b", [P, 3, 2 * P], F32, o4 + 1536)
        wr = sb("wr", [P, KT, LOG], F32, o4 + 1536)
        h_t = sb("h_t", [P, S], F32, o4 + 3840)
        o4 += 5888
        small = {}
        for name, n in (("gq", 2), ("gk", 2), ("g2c", KT), ("g2m", KT), ("sink", A_HEADS), ("eps", 2), ("ssx", 4), ("rsx", 4),
                        ("rx", 4), ("rqs", 4), ("rq", 4), ("mx", 4), ("negm", 4), ("den", 4), ("es", 4),
                        ("rden", 4), ("ssh", 16), ("ssum", 4), ("rh", 4), ("rb", LOG),
                        ("ramp4", 16), ("table", A_HEADS), ("rhs_", 4)):
            small[name] = sb(name, [P, n], F32, o4)
            o4 += -(-4 * n // 32) * 32
        wide = sb("wide", [P, ROWS, 3 * QC], F32, o4)
        assert o4 + 4 * ROWS * 3 * QC <= nc.sbuf_usable_end, o4
        gq, gk, g2c, g2m, sink, eps = (small[n] for n in ("gq", "gk", "g2c", "g2m", "sink", "eps"))
        ssx, rsx, rx, rqs, rq, mx, negm = (small[n] for n in ("ssx", "rsx", "rx", "rqs", "rq", "mx", "negm"))
        den, es, rden, ssh, ssum, rh = (small[n] for n in ("den", "es", "rden", "ssh", "ssum", "rh"))
        rb, ramp4, rhs_ = small["rb"], small["ramp4"], small["rhs_"]
        ident, ones, upper = mats[:, 0, :], mats[:, 1, :], mats[:, 2, :]
        onehot = sb("onehot", [BUCKETS, S], F32, R3 + 16 * K)
        mask_a = sb("mask_a", [A_HEADS, S], F32, R3 + 18 * K)
        tvec = sb("tvec", [A_HEADS, S], F32, R3 + 20 * K)
        o2 = R2
        rt = {}
        for name, shape in (("lgT", [LOG, S]), ("L", [P, NT, LOG]), ("gm", [P, 4]), ("gd", [P, 4, 4]), ("eg", [P, 4, 4]),
                            ("sgm", [P, 4]), ("pg", [P, 4]), ("gs", [P, 4, 4]), ("gx", [P, 4]), ("oh", [P, 4, 4]),
                            ("pen", [P, 4, 4]), ("em", [P, 4, 32]), ("v1", [P, 4]), ("d1", [P, 4, 32]),
                            ("s1", [P, 4, 32]), ("x1", [P, 4]), ("M12", [P, 2, 4, 32]), ("em2", [P, 4, 32]),
                            ("v2", [P, 4]), ("e2", [P, 4]), ("dn", [P, 4]), ("rr", [P, 4]), ("w12", [P, 2, 4]),
                            ("Ms", [P, 4, 32]), ("cnt", [P, 32]), ("nb", [P, 32]), ("nb2", [P, 32]),
                            ("xa", [P, 32]), ("xb", [P, 32]), ("xo", [P, 32]), ("cmp", [P, XTRA, 32]),
                            ("eidf", [P, XTRA]), ("pos", [P, 4, 32]), ("pr", [P, 2, 4, 32]), ("pk", [P, 8]),
                            ("ek", [P, 8]), ("xk", [P, 8]), ("blk", [P, 8]), ("blk2", [P, 8]), ("wi", [P, 8]),
                            ("tt", [P, 8]), ("isx", [P, 8]), ("item", [P, 8]),
                            ("nif", [P, 2]), ("ent", [P, 3, 8]), ("ramp", [P, 4, 32]), ("iota", [P, SLOTS]),
                            ("slot1h", [P, 8, P]), ("item1h", [P, 8, ITEMS]), ("entries", [P, 8, 3, ITEMS])):
            rt[name] = sb("r_" + name, shape, F32, o2)
            o2 += -(-4 * int(np.prod(shape[1:])) // 32) * 32
        eid = sb("eid", [P, XTRA], I32, o2 + 32)
        nitem = sb("nitem", [P, 2], I32, o2 + 96)
        assert o2 + 256 <= R3

        PS = ctx.enter_context(nc.psum_tensor("PS", [P, 8, S], F32))

        s_const, s_row, s_oh = sem("s_const"), sem("s_row"), sem("s_oh")
        s_x = [sem(f"s_x{t}") for t in range(NT)]
        s_raw = [sem(f"s_raw{i}") for i in range(RAW)]
        s_bias, s_bias_ready, s_tv, s_tvd = sem("s_bias"), sem("s_bias_ready"), sem("s_tv"), sem("s_tvd")
        s_whi, s_wlo, s_chunk = sem("s_whi"), sem("s_wlo"), sem("s_chunk")
        s_act, s_dve, s_pool, s_dve2 = sem("s_act"), sem("s_dve"), sem("s_pool"), sem("s_dve2")
        s_sp_passed, s_pool_passed, s_pe_passed = sem("s_sp_passed"), sem("s_pool_passed"), sem("s_pe_passed")
        s_eps, s_maskb, s_wide, s_wide_in = sem("s_eps"), sem("s_maskb"), sem("s_wide"), sem("s_wide_in")
        s_xsq, s_xn, s_xtr, s_xhi, s_xlo = (sem(n) for n in ("s_xsq", "s_xn", "s_xtr", "s_xhi", "s_xlo"))
        (s_tile, s_qhi, s_sqq, s_sqk, s_kg, s_rks, s_rqs, s_khi, s_vt, s_vhi, s_exp, s_pthi, s_ohi) = (
            sem(n) for n in ("s_tile", "s_qhi", "s_sqq", "s_sqk", "s_kg", "s_rks", "s_rqs", "s_khi", "s_vt", "s_vhi",
                             "s_exp", "s_pthi", "s_ohi"))
        (s_kn, s_klo, s_vlo, s_qlo, s_rq, s_negm, s_p, s_ptlo, s_olo) = (
            sem(n) for n in ("s_kn", "s_klo", "s_vlo", "s_qlo", "s_rq", "s_negm", "s_p", "s_ptlo", "s_olo"))
        (s_ksum, s_qsum, s_vtr, s_sc, s_ptr, s_pv) = (
            sem(n) for n in ("s_ksum", "s_qsum", "s_vtr", "s_sc", "s_ptr", "s_pv"))
        (s_sga, s_ta, s_sgb, s_mg, s_mhi, s_mlo) = (sem(n) for n in ("s_sga", "s_ta", "s_sgb", "s_mg", "s_mhi", "s_mlo"))
        (s_xres, s_h, s_hd, s_sqh, s_htr, s_htc, s_lg, s_wr, s_wrg) = (
            sem(n) for n in ("s_xres", "s_h", "s_hd", "s_sqh", "s_htr", "s_htc", "s_lg", "s_wr", "s_wrg"))
        (s_lgT, s_lgc, s_rh, s_M, s_pos, s_r1, s_r2, s_ent, s_tab, s_idx, s_cst2) = (
            sem(n) for n in ("s_lgT", "s_lgc", "s_rh", "s_M", "s_pos", "s_r1", "s_r2", "s_ent", "s_tab", "s_idx", "s_cst2"))
        s_wg = [sem(f"s_wg{c}") for c in range(4)]
        s_wu = [sem(f"s_wu{c}") for c in range(4)]
        s_wd = [sem(f"s_wd{c}") for c in range(4)]
        (s_gu, s_dn, s_gath, s_xs, s_xt2, s_xTc, s_sgm, s_hs, s_hst, s_hTc, s_yhi, s_ylo, s_comb, s_added, s_nreg) = (
            sem(n) for n in ("s_gu", "s_dn", "s_gath", "s_xs", "s_xt2", "s_xTc", "s_sgm", "s_hs", "s_hst", "s_hTc", "s_yhi",
                             "s_ylo", "s_comb", "s_added", "s_nreg"))
        (s_out, s_xg0) = (sem(n) for n in ("s_out", "s_xg0"))

        def settle(eng, passed):
            eng.sem_inc(passed, 1)

        win = w_in.rearrange("l (k p) c -> (l p) k c", p=P)
        upa = w_up_a.rearrange("l (k p) c -> (l p) k c", p=P)
        upb = w_up_b.rearrange("l (k p) c -> (l p) k c", p=P)
        wo = w_out.rearrange("l (k p) c -> (l p) k c", p=P)
        x_v = x.rearrange("b (t p) d -> p (b t) d", p=P)
        out_v = out.rearrange("b (t p) d -> p (b t) d", p=P)
        h_v = h_d.rearrange("(t p) d -> p t d", p=P)

        block = ctx.enter_context(nc.Block())

        @block.sync
        def _(sp):
            for t in range(NT):
                sp.dma_start(xt[:, t, :], x_v[:, t, :]).then_inc(s_x[t], 16)
                if t == 0:
                    sp.dma_start(gb[:], bass.AP(norm1_g.tensor, 0, [[0, P], [1, D]])).then_inc(s_row, 16)
                    sp.dma_start(mats[:], c_mats).then_inc(s_const, 16)

            def chunk(n, src):
                if not isinstance(n, int) or n >= RAW:
                    sp.wait_ge(s_wlo, n - (RAW - 1))
                    if not isinstance(n, int):
                        settle(sp, s_sp_passed)
                slot = chunk.slot % RAW
                chunk.slot += 1
                k = src.shape[1]
                sp.dma_start(w_raw[:, slot, :].rearrange("p (k c) -> p k c", k=k), src).then_inc(s_raw[slot], 16)

            chunk.slot = 0
            for n in range(RAW):
                chunk(n, win[:, 8 * (n % 2):8 * (n % 2) + 8, ds((COL_KA, COL_VA)[n // 2], P)])
            sp.wait_ge(s_tv, 1)
            sp.dma_start(tvec_d, tvec[:]).then_inc(s_tvd, 16)
            sp.wait_ge(s_tvd, 16)
            sp.dma_start(bias_d, bass.AP(tvec_d.tensor, P - 1, [[S, A_HEADS], [-1, P], [1, 3 * P]])).then_inc(s_tvd, 16)
            sp.dma_start(mask_b[:], c_maskb).then_inc(s_maskb, 16)

            def bias_a(hh):
                if hh:
                    sp.wait_ge(s_negm, hh)
                else:
                    sp.wait_ge(s_tvd, 32)
                sp.dma_start(bias[:, 0:2, :].rearrange("p a b -> p (a b)")[:, 0:3 * P], bias_d[hh]).then_inc(s_bias, 16)

            def bias_b(h_):
                if not isinstance(h_, int):
                    sp.wait_ge(s_bias_ready, h_)
                    settle(sp, s_sp_passed)
                sp.dma_start(wide[:].rearrange("p k c -> p (k c)"),
                             wide_d[ds(h_, 1), :, :].rearrange("o p c -> (o p) c")).then_inc(s_wide_in, 16)

            def spread(h_, r):
                sp.dma_start(wide_d[h_].rearrange("(i r) (k c) -> r k i c", r=ROWS, k=ROWS)[r],
                             bass.AP(rpb_pad.tensor, (h_ * (2 * NB_ROWS - 1) + NB_ROWS - 1 - r) * RPB_W + NB_COLS - 1,
                                     [[RPB_W, ROWS], [-1, QC], [1, 3 * QC]])).then_inc(s_wide, 16)

            n = 0
            for g in range(A_KV):
                cols = [COL_KA + HD * g, COL_VA + HD * g] + [COL_QA + HD * (A_GROUP * g + a) for a in range(A_GROUP)]
                for i, c in enumerate(cols):
                    for f in range(2):
                        if n >= RAW:
                            chunk(n, win[:, 8 * f:8 * f + 8, ds(c, P)])
                        if n >= 9 and (n - 9) % 12 in (0, 2, 4, 6):
                            bias_a(A_GROUP * ((n - 9) // 12) + (n - 9) % 12 // 2)
                        for i_ in range(3 * n, min(3 * n + 3, B_HEADS * ROWS)):
                            spread(i_ // ROWS, i_ % ROWS)
                        n += 1
            assert n == CH_B
            sp.wait_ge(s_wide, 16 * B_HEADS * ROWS)

            def b_head(h_, first):
                for i, c in enumerate((COL_QB, COL_KB, COL_VB)):
                    for f in range(2):
                        chunk(h_ * 6 + (CH_B + 2 * i + f), win[:, 8 * f:8 * f + 8, ds(h_ * HD + c, P)])
                        if first and f == 1 and i < 2:
                            bias_a(A_HEADS - 2 + i)
                        if i == 1 and f == 1:
                            bias_b(h_)

            b_head(0, True)
            with sp.Fori(1, B_HEADS) as h_:
                b_head(h_, False)
            with sp.Fori(0, KT) as j:
                n = j * 6 + CH_M
                c = j * P
                chunk(n, win[:, 0:8, ds(c + COL_GA, P)])
                chunk(n + 1, win[:, 8:16, ds(c + COL_GA, P)])
                chunk(n + 2, upa[:, :, ds(c, P)])
                chunk(n + 3, win[:, 0:8, ds(c + COL_GB, P)])
                chunk(n + 4, win[:, 8:16, ds(c + COL_GB, P)])
                chunk(n + 5, upb[:, :, ds(c, P)])

            wg_v = w_gate.rearrange("l e (p k) f -> p (l e) k f", p=P)
            wu_v = w_up.rearrange("l e (p k) f -> p (l e) k f", p=P)
            wd_v = w_down.rearrange("l e (j p c) n -> p (l e) j c n", j=2, p=P)

            def load_gate(e, c):
                sp.dma_start(wg_s[:, 4 * c:4 * c + 4, :], wg_v[:, ds(e, 1), 4 * c:4 * c + 4, :].rearrange("p o k f -> p (o k) f")).then_inc(s_wg[c], 16)

            def load_up(e, c):
                sp.dma_start(wu_s[:, 4 * c:4 * c + 4, :], wu_v[:, ds(e, 1), 4 * c:4 * c + 4, :].rearrange("p o k f -> p (o k) f")).then_inc(s_wu[c], 16)

            def load_down(e, c):
                sp.dma_start(wd_s[:, c, :], wd_v[:, ds(e, 1), c // 2, c % 2, :].rearrange("p o n -> p (o n)")).then_inc(s_wd[c], 16)

            for nn in range(NT):
                for c in range(8):
                    chunk(CH_O + 8 * nn + c, wo[:, 2 * c:2 * c + 2, nn * S:nn * S + S])
                    if nn == 0 and c == 2:
                        sp.wait_ge(s_bias_ready, B_HEADS)
                        wr3 = wr[:]
                        sp.dma_start(wr3[:, :, 0:GROUPS],
                                     w_router_group.rearrange("l (k p) c -> (l p) k c", p=P)).then_inc(s_wr, 16)
                        sp.dma_start(wr3[:, :, GROUPS:LOG],
                                     w_router_expert.rearrange("l (k p) c -> (l p) k c", p=P)).then_inc(s_wr, 16)
                        sp.wait_ge(s_chunk, CH_O)
                    if nn == 0 and 4 <= c:
                        load_gate(0, c - 4)
                    if c == 3:
                        if nn:
                            sp.wait_ge(s_h, 4 * nn)
                        else:
                            sp.wait_ge(s_mg, KT)
                        sp.dma_start(x_res[:], x_v[:, 0:3, nn * S:nn * S + S]).then_inc(s_xres, 16)
                        sp.dma_start(x_last[:], x_v[:, 3, nn * S:nn * S + S]).then_inc(s_xres, 16)
                        if nn:
                            sp.dma_start(h_v[:, :, (nn - 1) * S:nn * S], h[:, :, (nn - 1) * S:nn * S]).then_inc(s_hd, 16)
                    if nn == 1 and 4 <= c:
                        if c == 4:
                            sp.wait_ge(s_mlo, KT)
                        load_up(0, c - 4)
            for nn in range(NT - 1, NT):
                sp.wait_ge(s_h, 4 * nn + 4)
                sp.dma_start(h_v[:, :, nn * S:nn * S + S], h[:, :, nn * S:nn * S + S]).then_inc(s_hd, 16)
            for c in range(4):
                load_down(0, c)

            def item_loads(e, i):
                for c in range(4):
                    sp.wait_ge(s_gu, i * 4 + (c - 3))
                    settle(sp, s_sp_passed)
                    load_gate(e, c)
                    load_up(e, c)
                for c in range(4):
                    sp.wait_ge(s_dn, i * 4 + (c - 3))
                    settle(sp, s_sp_passed)
                    load_down(e, c)

            with sp.Fori(1, EXPERTS) as i:
                item_loads(i, i)
            sp.wait_ge(s_r2, 1)
            extra = sp.value_load(nitem[0:1, 1:2], min_val=0, max_val=XTRA)
            with sp.If(extra > 0):
                with sp.Fori(0, extra) as i:
                    e = sp.value_load(eid[0:1, ds(i, 1)], min_val=0, max_val=EXPERTS - 1)
                    item_loads(e, i + EXPERTS)
            items = sp.value_load(nitem[0:1, 0:1], min_val=EXPERTS, max_val=EXPERTS + XTRA)
            for t in range(NT):
                sp.wait_ge(s_added, items * 8 + (2 * t + 4))
                settle(sp, s_sp_passed)
                sp.dma_start(out_v[:, t, :], h[:, t, :]).then_inc(s_out, 16)
            sp.wait_ge(s_out, 16 * NT)

        @block.gpsimd
        def _(pool):
            pool.memset(eps[:, 0:1], EPS).then_inc(s_eps, 1)
            pool.memset(eps[:, 1:2], EPS * HD).then_inc(s_eps, 1)
            gp = pool
            gp.dma_start(onehot[:], c_onehot).then_inc(s_oh, 16)
            gp.dma_start(mask_a[:], c_maska).then_inc(s_oh, 16)
            gp.dma_start(small["table"][0:BUCKETS, :], rel_bias_table).then_inc(s_oh, 16)
            for i, (qn, kk) in enumerate(((q_norm_a, k_norm_a), (q_norm_b, k_norm_b))):
                gp.dma_start(gq[:, i:i + 1], qn.rearrange("l d -> d l"), allow_slow_non_contiguous=True).then_inc(s_cst2, 16)
                gp.dma_start(gk[:, i:i + 1], kk.rearrange("l d -> d l"), allow_slow_non_contiguous=True).then_inc(s_cst2, 16)
            gp.dma_start(sink[:], bass.AP(sink_a.tensor, 0, [[0, P], [1, A_HEADS]])).then_inc(s_cst2, 16)
            gp.dma_start(g2m[:], norm2_g.rearrange("l (p k) -> (l p) k", p=P)).then_inc(s_wrg, 16)
            gp.dma_start(g2c[:], norm2_g.rearrange("l (k p) -> (l p) k", p=P), allow_slow_non_contiguous=True).then_inc(s_wrg, 16)
            gp.dma_start(rb[:, 0:GROUPS], bass.AP(b_router_group.tensor, 0, [[0, P], [1, GROUPS]])).then_inc(s_wrg, 16)
            gp.dma_start(rb[:, GROUPS:LOG], bass.AP(b_router_expert.tensor, 0, [[0, P], [1, EXPERTS]])).then_inc(s_wrg, 16)
            gp.dma_start(ramp4[:], c_ramp[:, 0:16]).then_inc(s_wrg, 16)
            pool.wait_ge(s_maskb, 16)
            with pool.Fori(0, B_HEADS) as h_:
                pool.wait_ge(s_wide_in, h_ * 16 + 16)
                pool.wait_ge(s_negm, h_ + A_HEADS)
                for kind in range(3):
                    ins = nc.gpsimd.tensor_tensor(bias[:, kind, :].rearrange("p (c k) -> p k c", k=ROWS),
                                                  wide[:, :, QC - 8 * kind:QC - 8 * kind + KC],
                                                  mask_b[:, kind, :].rearrange("p (k c) -> p k c", k=ROWS), ALU.add)
                ins.then_inc(s_bias_ready, 1)
            pool.wait_ge(s_wlo, CH_END)
            pool.wait_ge(s_chunk, CH_END)
            pool.wait_ge(s_h, 4 * NT)
            gp.dma_start(rt["ramp"][:].rearrange("p a b -> p (a b)"), c_ramp[:, 32:32 + 128]).then_inc(s_idx, 16)
            gp.dma_start(rt["iota"][:], c_ramp[:, 160:160 + SLOTS]).then_inc(s_idx, 16)
            gp.dma_start(rt["ent"][:].rearrange("p a b -> p (a b)"), c_entry).then_inc(s_idx, 16)
            gp.dma_start(token[:], c_tokens).then_inc(s_idx, 16)
            nc.gpsimd.memset(xg[:], 0.0).then_inc(s_xg0, 1)
            pool.wait_ge(s_r1, 1)
            items = pool.value_load(nitem[0:1, 0:1], min_val=EXPERTS, max_val=EXPERTS + XTRA)
            pool.wait_ge(s_hd, 16 * NT)
            pool.wait_ge(s_xg0, 1)
            pool.wait_ge(s_nreg, 1)

            nc.gpsimd.tensor_copy(cur_x[:], idx_x[:, 0:1]).then_inc(s_pool, 1)
            pool.wait_ge(s_pool, 1)
            gp.indirect_dma_start(xg[:], None, h_d, bass.IndirectOffsetOnAxis(ap=cur_x[:, 0:1], axis=0),
                                  bounds_check=S - 1, oob_is_err=False).then_inc(s_gath, 16)
            with pool.Fori(0, items) as i:
                pool.wait_ge(s_gath, i * 16 + 16)
                nc.gpsimd.tensor_copy(cur_x[:], idx_x[:, ds(i + 1, 1)]).then_inc(s_pool, 1)
                pool.wait_ge(s_pool, i + 2)
                pool.wait_ge(s_xt2, i + 1)
                settle(pool, s_pool_passed)
                gp.indirect_dma_start(xg[:], None, h_d, bass.IndirectOffsetOnAxis(ap=cur_x[:, 0:1], axis=0),
                                      bounds_check=S - 1, oob_is_err=False).then_inc(s_gath, 16)

        def grid(ap, kind):
            return ap if kind == 0 else ap.rearrange("p (r c) -> p r c", r=ROWS)

        def tokens(buf, kind):
            return buf[:] if kind == 0 else buf[:].rearrange("p (c r) -> p r c", r=ROWS)

        def o_view(buf, hh, kind):
            v = buf[:, ds(hh, 1), :]
            if kind == 0:
                return v.rearrange("p o c -> p (o c)")
            return v.rearrange("p o (r c) -> p (o c) r", r=ROWS)

        def o_psum(kind):
            return PS[:, 6, :] if kind == 0 else PS[:, 6, :].rearrange("p (c r) -> p c r", r=ROWS)

        @block.scalar
        def _(act):
            own = Chain(act, s_act)
            act_fn = nc.scalar.activation
            act.wait_ge(s_eps, 2)
            for t in range(NT):
                act.wait_ge(s_x[t], 16)
                own.do(act_fn(junk[:], xt[:, t, :], ACT.Square, accum_out=ssx[:, t:t + 1]))
                act_fn(rsx[:, t:t + 1], ssx[:, t:t + 1], ACT.Sqrt, bias=eps[:, 0:1], scale=1.0 / D).then_inc(s_xsq, 1)
            for G in range(16):
                t, kk = G // 4, G % 4
                act.wait_ge(s_xtr, G + 1)
                act_fn(x_hi[:, 4 * kk:4 * kk + 4, t * P:t * P + P],
                       PS[:, G % 8, :].rearrange("p (k c) -> p k c", k=4), ACT.Copy).then_inc(s_xhi, 1)
            def split(n, python_n):
                r, b = python_n % RAW, python_n % SPLIT
                act.wait_ge(s_raw[r], (n - r) // RAW * 16 + 16 if isinstance(n, int) else split.raw(n, r))
                if not isinstance(n, int) or n >= SPLIT:
                    act.wait_ge(s_chunk, n - (SPLIT - 1))
                act_fn(w_hi[:, b, :], w_raw[:, r, :], ACT.Copy).then_inc(s_whi, 1)

            def q_tile(hh, bank, kind, need, vtr, first=False):
                act.wait_ge(s_chunk, need)
                if not first:
                    act.wait_ge(s_sc, hh)
                act_fn(tokens(q_hi, kind), grid(PS[:, bank, :], kind), ACT.Copy,
                       scale=gq[:, kind:kind + 1]).then_inc(s_qhi, 1)
                act.wait_ge(s_vtr, vtr)
                if not first:
                    act.wait_ge(s_qsum, hh)
                act_fn(tokens(sq, kind), grid(PS[:, bank, :], kind), ACT.Square).then_inc(s_sqq, 1)

            def q_root(hh, kind, first=False):
                act.wait_ge(s_qsum, hh + 1)
                if not first:
                    act.wait_ge(s_rq, hh)
                col = PS[:, 7 if kind == 0 else 4, 0:4]
                act_fn(rqs[:], col, ACT.Sqrt, bias=eps[:, 1:2]).then_inc(s_rqs, 1)

            def k_tile(kv, hh, bank, kind, need, first=False):
                act.wait_ge(s_chunk, need)
                if not first:
                    act.wait_ge(s_klo, kv)
                    act.wait_ge(s_qsum, hh)
                act_fn(kn[:], PS[:, bank, :], ACT.Copy, scale=gk[:, kind:kind + 1]).then_inc(s_kg, 1)
                act_fn(sq[:], PS[:, bank, :], ACT.Square).then_inc(s_sqk, 1)

            def k_root(kv, bank, p_used):
                act.wait_ge(s_ksum, kv + 1)
                if p_used is not None:
                    act.wait_ge(s_ptr, p_used)
                act_fn(rk[:], PS[:, bank, :], ACT.Sqrt, bias=eps[:, 0:1], scale=1.0 / HD).then_inc(s_rks, 1)

            def k_split(kv, kind, sc_used):
                act.wait_ge(s_kn, kv + 1)
                if sc_used is not None:
                    act.wait_ge(s_sc, sc_used)
                act_fn(tokens(k_hi, kind), grid(kn[:], kind), ACT.Copy).then_inc(s_khi, 1)

            def v_tile(kv, kind, bank, need):
                act.wait_ge(s_chunk, need)
                act.wait_ge(s_ksum, kv + 1)
                act_fn(tokens(vt, kind), grid(PS[:, bank, :], kind), ACT.Copy).then_inc(s_vt, 1)

            def v_split(kv, src, pv_used):
                act.wait_ge(s_vtr, kv + 1)
                if pv_used is not None:
                    act.wait_ge(s_pv, pv_used)
                n = src.shape[1]
                act_fn(v_hi[:, 0:n // P, :].rearrange("p a b -> p (a b)"), src, ACT.Copy).then_inc(s_vhi, 1)

            def exps(hh, kind, bias_col):
                act.wait_ge(s_negm, hh + 1)
                for b in range(NT):
                    lo, hi = a_keys(b) if kind == 0 else (0, 2 * P)
                    ins = act_fn(prob[:, b, lo:hi], prob[:, b, lo:hi], ACT.Exp, bias=negm[:, b:b + 1],
                                 accum_out=den[:, b:b + 1])
                    if kind or b < NT - 1:
                        ins.then_inc(s_exp, 1)
                if kind == 0:
                    act_fn(es[:], negm[:], ACT.Exp, bias=bias_col).then_inc(s_exp, 1)

            def pt_split(hh, kind, first=False):
                act.wait_ge(s_ptr, hh + 1)
                if not first:
                    act.wait_ge(s_pv, hh)
                if kind == 0:
                    act_fn(pt_hi[:, 0, P:3 * P], PS[:, 2, P:3 * P], ACT.Copy)
                    act_fn(pt_hi[:, 3, 0:2 * P], PS[:, 5, 0:2 * P], ACT.Copy)
                    act_fn(pt_hi[:, 1:3, :], PS[:, 3:5, 0:3 * P], ACT.Copy).then_inc(s_pthi, 1)
                else:
                    act_fn(pt_hi[:, :, 0:2 * P], PS[:, 4:6, :].rearrange("p a (b c) -> p (a b) c", b=2),
                           ACT.Copy).then_inc(s_pthi, 1)

            def o_split(hh, kind):
                act.wait_ge(s_pv, hh + 1)
                act_fn(o_view(o_hi, hh, kind), o_psum(kind), ACT.Copy).then_inc(s_ohi, 1)

            act.wait_ge(s_xlo, 16)
            act.wait_ge(s_cst2, 5 * 16)
            split(0, 0)
            for g in range(A_KV):
                for s in range(12):
                    n = 12 * g + s
                    split(n + 1, n + 1)
                    tail_head = A_GROUP * g - 1
                    if s == 0 and g:
                        q_tile(tail_head, 1, 0, n, g)
                        pt_split(tail_head - 1, 0)
                    if s == 1 and g:
                        o_split(tail_head - 1, 0)
                        q_root(tail_head, 0)
                        exps(tail_head, 0, sink[:, tail_head:tail_head + 1])
                    if s == 2:
                        k_tile(g, A_GROUP * g, 0, 0, n, first=(g == 0))
                        if g:
                            pt_split(tail_head, 0)
                    if s == 3:
                        if g:
                            o_split(tail_head, 0)
                        k_root(g, 7, A_GROUP * g if g else None)
                    if s == 4:
                        k_split(g, 0, A_GROUP * g if g else None)
                        v_tile(g, 0, 1, n)
                    if s == 5:
                        v_split(g, PS[:, 7, :], A_GROUP * g if g else None)
                    if s >= 6 and s % 2 == 0:
                        a = (s - 6) // 2
                        hh = A_GROUP * g + a
                        q_tile(hh, a % 2, 0, n, g + 1, first=(hh == 0))
                        if a:
                            pt_split(hh - 1, 0, first=(hh == 1))
                    if s >= 7 and s % 2 == 1:
                        a = (s - 7) // 2
                        hh = A_GROUP * g + a
                        if a:
                            o_split(hh - 1, 0)
                        q_root(hh, 0, first=(hh == 0))
                        exps(hh, 0, sink[:, hh:hh + 1])
            split.raw = lambda n, r: None

            def b_steps(h_, first):
                hh = h_ + A_HEADS
                kv = h_ + A_KV
                c0 = h_ * 6 + CH_B
                for s in range(6):
                    nxt = s + 1
                    split.raw = lambda n, r, nxt=nxt: h_ * 32 + (16 * ((CH_B + nxt - r) // RAW) + 16)
                    split(c0 + nxt, CH_B + nxt)
                    if s == 0:
                        if first:
                            q_tile(A_HEADS - 1, 1, 0, c0, A_KV)
                            pt_split(A_HEADS - 2, 0)
                        else:
                            k_split(kv - 1, 1, hh - 1)
                            v_tile(kv - 1, 1, 7, c0)
                    if s == 1:
                        if first:
                            o_split(A_HEADS - 2, 0)
                            q_root(A_HEADS - 1, 0)
                            exps(A_HEADS - 1, 0, sink[:, A_HEADS - 1:A_HEADS])
                        else:
                            v_split(kv - 1, PS[:, 4:6, :].rearrange("p a b -> p (a b)"), hh - 1)
                            exps(hh - 1, 1, None)
                    if s == 2:
                        q_tile(hh, 0, 1, c0 + 2, kv)
                        pt_split(hh - 1, 0 if first else 1)
                    if s == 3:
                        o_split(hh - 1, 0 if first else 1)
                        q_root(hh, 1)
                    if s == 4:
                        k_tile(kv, hh + 1, 1, 1, c0 + 4)
                    if s == 5:
                        k_root(kv, 6, hh)

            b_steps(0, True)
            with act.Fori(1, B_HEADS) as h_:
                b_steps(h_, False)

            def m_steps(j, first):
                c0 = j * 6 + CH_M
                hh, kv = HEADS, A_KV + B_HEADS
                for s in range(6):
                    nxt = s + 1
                    split.raw = lambda n, r, nxt=nxt: j * 32 + (16 * ((CH_M + nxt - r) // RAW) + 16)
                    split(c0 + nxt, CH_M + nxt)
                    if first and s == 0:
                        k_split(kv - 1, 1, hh - 1)
                        v_tile(kv - 1, 1, 7, c0)
                    if first and s == 1:
                        v_split(kv - 1, PS[:, 4:6, :].rearrange("p a b -> p (a b)"), hh - 1)
                        exps(hh - 1, 1, None)
                    if first and s == 2:
                        pt_split(hh - 1, 1)
                        act.wait_ge(s_vtr, kv)
                        act.wait_ge(s_qsum, hh)
                    if s == 2:
                        if not first:
                            act.wait_ge(s_ta, j)
                        act.wait_ge(s_chunk, c0 + 2)
                        act_fn(sig_a[:], PS[:, 0, :], ACT.Sigmoid).then_inc(s_sga, 1)
                    if first and s == 3:
                        o_split(hh - 1, 1)
                    if s == 5:
                        if not first:
                            act.wait_ge(s_mg, j)
                        act.wait_ge(s_chunk, c0 + 5)
                        act_fn(sig_b[:], PS[:, 7, :], ACT.Sigmoid).then_inc(s_sgb, 1)

            m_steps(0, True)
            with act.Fori(1, KT) as j:
                m_steps(j, False)

            def merged_split(j):
                act.wait_ge(s_mg, j + 1)
                act_fn(m_hi[:, j, :], m_raw[:, j, :], ACT.Copy).then_inc(s_mhi, 1)

            act.wait_ge(s_chunk, CH_O - 1)
            merged_split(0)
            merged_split(1)

            def h_squares(nn):
                for t in range(NT):
                    act.wait_ge(s_h, 4 * nn + t + 1)
                    if nn or t:
                        act.wait_ge(s_sqh, 4 * nn + t)
                    act_fn(PS[:, 6, :], h[:, t, nn * S:nn * S + S], ACT.Square,
                           accum_out=ssh[:, 4 * t + nn:4 * t + nn + 1]).then_inc(s_sqh, 1)

            def h_copy(k):
                act.wait_ge(s_htr, k + 1)
                if k:
                    act.wait_ge(s_lg, k)
                act_fn(h_t[:], PS[:, 4 + k % 2, :], ACT.Copy).then_inc(s_htc, 1)

            for nn in range(NT):
                for c in range(8):
                    n = CH_O + 8 * nn + c
                    if n + 1 < CH_END:
                        split(n + 1, n + 1)
                    if nn == 0 and c < 7:
                        merged_split(2 * c + 2)
                        merged_split(2 * c + 3)
                    if nn and c == 0:
                        h_squares(nn - 1)
                    if nn and 2 <= c < 6:
                        h_copy(4 * (nn - 1) + c - 2)
            h_squares(NT - 1)
            for k in range(4 * NT - 4, 4 * NT):
                h_copy(k)
            act.wait_ge(s_M, 1)
            act_fn(rhs_[:], ssum[:], ACT.Sqrt, bias=eps[:, 0:1], scale=1.0 / D).then_inc(s_rh, 1)
            act.wait_ge(s_lg, 4 * NT)
            act_fn(rt["lgT"][:], PS[0:LOG, 7, :], ACT.Copy).then_inc(s_lgc, 1)
            act.wait_ge(s_M, 2)
            act_fn(rt["eg"][:], rt["gd"][:], ACT.Exp).then_inc(s_lgc, 1)
            act.wait_ge(s_M, 3)
            act_fn(rt["e2"][:], rt["e2"][:], ACT.Exp).then_inc(s_lgc, 1)
            act.wait_ge(s_r1, 1)
            items = act.value_load(nitem[0:1, 0:1], min_val=EXPERTS, max_val=EXPERTS + XTRA)
            act.wait_ge(s_nreg, 1)

            def rows_scaled(i, first):
                act.wait_ge(s_gath, i * 16 + 16)
                act_fn(xg[:], xg[:], ACT.Copy, scale=tab[0:SLOTS, 2, ds(i, 1)]).then_inc(s_xs, 1)

            rows_scaled(0, True)
            with act.Fori(0, items) as i:
                rows_scaled(i + 1, False)
                act.wait_ge(s_gu, i * 4 + 4)
                act_fn(sg[:], PS[:, 0, 0:F // 2], ACT.Sigmoid).then_inc(s_sgm, 1)
                act.wait_ge(s_dn, i * 4 + 4)
                act.wait_ge(s_comb, i * 8 + 8)
                act_fn(y_hi[:], PS[:, 4:6, :].rearrange("p a b -> p (a b)"), ACT.Copy,
                       scale=tab[:, 1, ds(i, 1)]).then_inc(s_yhi, 1)

        def routing(dve, own, V):
            R = {k: v for k, v in rt.items()}
            a = {k: v[:] for k, v in rt.items()}
            tt, ts, stt = V.tensor_tensor, V.tensor_scalar, V.scalar_tensor_tensor

            def top(sc, best, ramp, sel, n, tmp_score, tmp_max):
                own.do(V.reduce_max(best, sc, AX))
                own.do(tt(tmp_score, sc, bc(best, n), ALU.subtract))
                own.do(stt(out=tmp_score, in0=tmp_score, scalar=0.0, in1=ramp, op0=ALU.is_equal, op1=ALU.mult))
                own.do(V.reduce_max(tmp_max, tmp_score, AX))
                own.do(tt(sel, tmp_score, bc(tmp_max, n), ALU.is_equal))

            dve.wait_ge(s_sqh, 16)
            V.reduce_sum(ssum[:], ssh[:].rearrange("p (t n) -> p t n", t=NT), AX).then_inc(s_M, 1)
            dve.wait_ge(s_rh, 1)
            own.do(V.reciprocal(rh[:], rhs_[:]))
            dve.wait_ge(s_idx, 64)
            for k in range(2):
                own.do(V.tensor_copy(R["ent"][:, 2, 4 * k:4 * k + 4], rh[:]))
            dve.wait_ge(s_lgT, 1)
            for t in range(NT):
                own.link(stt(out=R["L"][:, t, :], in0=PS[:, 0, t * LOG:t * LOG + LOG], scalar=rh[:, t:t + 1], in1=rb[:],
                             op0=ALU.mult, op1=ALU.add))
            own.wait()
            g = R["L"][:, :, 0:GROUPS]
            e = R["L"][:, :, GROUPS:LOG].rearrange("p t (g e) -> p t g e", g=GROUPS)
            ramp4v = ramp4[:].rearrange("p (t g) -> p t g", t=NT)
            own.do(V.reduce_max(a["gm"], g, AX))
            tt(a["gd"], g, bc(a["gm"], 4), ALU.subtract).then_inc(s_M, 1)
            dve.wait_ge(s_M, 2)
            own.do(stt(out=a["gs"], in0=a["gd"], scalar=0.0, in1=ramp4v, op0=ALU.is_equal, op1=ALU.mult))
            own.do(V.reduce_max(a["gx"], a["gs"], AX))
            own.do(tt(a["oh"], a["gs"], bc(a["gx"], 4), ALU.is_equal))
            own.do(ts(a["pen"], a["oh"], -1.0, -NEG, ALU.add, ALU.mult))
            own.do(tt(a["em"].rearrange("p t (g e) -> p t g e", g=GROUPS), e, bc(a["pen"], PER_GROUP), ALU.add))
            M1, M2 = R["M12"][:, 0, :, :], R["M12"][:, 1, :, :]
            top(a["em"], a["v1"], a["ramp"], M1, 32, a["s1"], a["x1"])
            own.do(stt(out=a["em2"], in0=M1, scalar=2 * NEG, in1=a["em"], op0=ALU.mult, op1=ALU.add))
            top(a["em2"], a["v2"], a["ramp"], M2, 32, a["s1"], a["x1"])
            own.do(tt(a["e2"], a["v2"], a["v1"], ALU.subtract))
            dve.sem_inc(s_M, 1)
            tt(a["Ms"], M1, M2, ALU.add).then_inc(s_M, 1)
            dve.wait_ge(s_lgc, 3)
            own.do(V.reduce_sum(a["sgm"], a["eg"], AX))
            own.do(V.reciprocal(a["pg"], a["sgm"]))
            own.do(ts(a["dn"], a["e2"], 1.0, None, ALU.add))
            own.do(V.reciprocal(a["rr"], a["dn"]))
            own.do(tt(R["w12"][:, 0, :], a["pg"], a["rr"], ALU.mult))
            own.do(tt(R["w12"][:, 1, :], R["w12"][:, 0, :], a["e2"], ALU.mult))
            own.do(V.tensor_copy(R["ent"][:, 1, :], a["w12"].rearrange("p k t -> p (k t)")))
            dve.wait_ge(s_pos, 2)
            own.do(V.tensor_copy(a["cnt"], PS[:, 1, 128:160]))
            own.do(V.tensor_copy(a["pos"].rearrange("p t e -> p (t e)"), PS[:, 1, 0:128]))
            own.do(ts(a["nb"], a["cnt"], float(SLOTS), None, ALU.is_gt))
            src, dst = "nb", "nb2"
            for m in range(2, MORE + 1):
                own.do(stt(out=a[dst], in0=a["cnt"], scalar=float(SLOTS * m), in1=a[src], op0=ALU.is_gt, op1=ALU.add))
                src, dst = dst, src
            nb = src
            own.do(V.tensor_copy(a["xa"], a[nb]))
            src, dst = "xa", "xb"
            for sh in (1, 2, 4, 8, 16):
                own.do(V.tensor_copy(R[dst][:, 0:sh], R[src][:, 0:sh]))
                own.do(tt(R[dst][:, sh:32], R[src][:, sh:32], R[src][:, 0:32 - sh], ALU.add))
                src, dst = dst, src
            xi = src
            own.do(tt(a["xo"], a[xi], a[nb], ALU.subtract))
            own.do(ts(R["nif"][:, 0:1], R[xi][:, 31:32], float(EXPERTS), None, ALU.add))
            own.do(V.tensor_copy(R["nif"][:, 1:2], R[xi][:, 31:32]))
            V.tensor_copy(nitem[:], a["nif"]).then_inc(s_r1, 1)
            own.do(tt(a["cmp"], rep(a[xi], XTRA), bc(R["iota"][:, 0:XTRA], EXPERTS), ALU.is_le))
            own.do(V.reduce_sum(a["eidf"], a["cmp"], AX))
            own.do(ts(a["eidf"], a["eidf"], float(EXPERTS - 1), None, ALU.min))
            V.tensor_copy(eid[:], a["eidf"]).then_inc(s_r2, 1)
            M = a["M12"].rearrange("p k t e -> p (k t) e")
            prf = a["pr"].rearrange("p k t e -> p (k t) e")
            for k in range(2):
                own.link(tt(R["pr"][:, k, :, :], R["M12"][:, k, :, :], a["pos"], ALU.mult))
            own.wait()
            own.do(V.reduce_sum(a["pk"], prf, AX))
            own.do(tt(prf, M, rep(a["iota"][:, 0:EXPERTS], 8), ALU.mult))
            own.do(V.reduce_sum(a["ek"], prf, AX))
            own.do(tt(prf, M, rep(a["xo"], 8), ALU.mult))
            own.do(V.reduce_sum(a["xk"], prf, AX))
            own.do(ts(a["blk"], a["pk"], float(SLOTS), None, ALU.is_ge))
            src, dst = "blk", "blk2"
            for m in range(2, MORE + 1):
                own.do(stt(out=a[dst], in0=a["pk"], scalar=float(SLOTS * m), in1=a[src], op0=ALU.is_ge, op1=ALU.add))
                src, dst = dst, src
            b = a[src]
            own.do(stt(out=a["wi"], in0=b, scalar=-float(SLOTS), in1=a["pk"], op0=ALU.mult, op1=ALU.add))
            own.do(ts(a["isx"], b, 0.0, None, ALU.is_gt))
            own.do(tt(a["tt"], a["xk"], b, ALU.add))
            own.do(stt(out=a["tt"], in0=a["tt"], scalar=float(EXPERTS - 1), in1=a["ek"], op0=ALU.add, op1=ALU.subtract))
            own.do(tt(a["tt"], a["tt"], a["isx"], ALU.mult))
            own.do(tt(a["item"], a["tt"], a["ek"], ALU.add))
            wi3 = bass.AP(a["wi"].tensor, a["wi"].offset, [list(x) for x in a["wi"].ap] + [[0, 2], [0, SLOTS]])
            io3 = bass.AP(a["iota"].tensor, a["iota"].offset, [list(a["iota"].ap[0]), [0, 8], [0, 2], [1, SLOTS]])
            own.link(tt(a["slot1h"].rearrange("p j (f s) -> p j f s", f=2), io3, wi3, ALU.is_equal))
            own.do(tt(a["item1h"], rep(a["iota"][:, 0:ITEMS], 8), bc(a["item"], ITEMS), ALU.is_equal))
            for c in range(3):
                ins = tt(R["entries"][:, :, c, :], a["item1h"], bc(R["ent"][:, c, :], ITEMS), ALU.mult)
            ins.then_inc(s_ent, 1)
            dve.wait_ge(s_tab, 1)
            tab_ps = PS[:, 0, 0:3 * ITEMS].rearrange("p (c i) -> p c i", c=3)
            own.do(ts(idx_x[:], tab_ps[0:SLOTS, 0, :], 2.0 * S, None, ALU.add))
            own.do(ts(tab[:, 0, :], tab_ps[:, 0, :], 2.0 * S, None, ALU.add))
            own.do(V.tensor_copy(tab[:, 1:3, :], tab_ps[:, 1:3, :]))
            dve.sem_inc(s_nreg, 1)

        @block.vector
        def _(dve):
            own = Chain(dve, s_dve)
            V = nc.vector
            for t in range(NT):
                dve.wait_ge(s_xsq, t + 1)
                if t == 0:
                    dve.wait_ge(s_row, 16)
                own.do(V.reciprocal(rx[:, t:t + 1], rsx[:, t:t + 1]))
                V.scalar_tensor_tensor(out=xt[:, t, :], in0=xt[:, t, :], scalar=rx[:, t:t + 1], in1=gb[:],
                                       op0=ALU.mult, op1=ALU.mult).then_inc(s_xn, 1)
            for G in range(16):
                t, kk = G // 4, G % 4
                dve.wait_ge(s_xhi, G + 1)
                hi = x_hi[:, 4 * kk:4 * kk + 4, t * P:t * P + P].bitcast(F32)
                V.tensor_tensor(x_lo[:, 4 * kk:4 * kk + 4, t * P:t * P + P],
                                PS[:, G % 8, :].rearrange("p (k c) -> p k c", k=4), hi, ALU.subtract).then_inc(s_xlo, 1)
            dve.wait_ge(s_pos, 1)
            V.tensor_tensor(tvec[:], PS[0:A_HEADS, 7, :], mask_a[:], ALU.add).then_inc(s_tv, 1)

            def split(n, python_n):
                r, b = python_n % RAW, python_n % SPLIT
                dve.wait_ge(s_whi, n + 1)
                V.tensor_tensor(w_lo[:, b, :], w_raw[:, r, :], w_hi[:, b, :].bitcast(F32), ALU.subtract).then_inc(s_wlo, 1)

            def q_tile(hh, bank, kind):
                dve.wait_ge(s_qhi, hh + 1)
                dve.wait_ge(s_sqq, hh + 1)
                V.scalar_tensor_tensor(out=tokens(q_lo, kind), in0=grid(PS[:, bank, :], kind),
                                       scalar=gq[:, kind:kind + 1], in1=tokens(q_hi, kind).bitcast(F32), op0=ALU.mult, op1=ALU.subtract).then_inc(s_qlo, 1)

            def softmax(hh, kind, hcol):
                dve.wait_ge(s_rqs, hh + 1)
                V.reciprocal(rq[:], rqs[:]).then_inc(s_rq, 1)
                dve.wait_ge(s_rq, hh + 1)
                dve.wait_ge(s_sc, hh + 1)
                if kind == 0:
                    dve.wait_ge(s_bias, (hh + 1) * 16)
                else:
                    dve.wait_ge(s_bias_ready, hh - (A_HEADS - 1))
                for b in range(NT):
                    lo, hi = a_keys(b) if kind == 0 else (0, 2 * P)
                    if kind == 0:
                        src, bs = PS[:, 2 + b, lo:hi], bias[:, 0:2, :].rearrange("p a b -> p (a b)")[:, lo:hi]
                    else:
                        src, bs = PS[:, 2 + b // 2, (b % 2) * 256:(b % 2) * 256 + 256], bias[:, B_KIND[b], :]
                    own.link(V.scalar_tensor_tensor(out=prob[:, b, lo:hi], in0=src, scalar=rq[:, b:b + 1], in1=bs,
                                                    op0=ALU.mult, op1=ALU.add))
                for b in range(NT):
                    lo, hi = a_keys(b) if kind == 0 else (0, 2 * P)
                    own.wait(3)
                    own.link(V.reduce_max(mx[:, b:b + 1], prob[:, b, lo:hi], AX))
                own.wait()
                if kind == 0:
                    V.tensor_scalar(negm[:], mx[:], hcol, -1.0, ALU.max, ALU.mult).then_inc(s_negm, 1)
                else:
                    V.tensor_scalar(negm[:], mx[:], -1.0, None, ALU.mult).then_inc(s_negm, 1)

            def normalise(hh, kind):
                dve.wait_ge(s_exp, (hh + 1) * 4)
                if kind == 0:
                    own.do(V.tensor_tensor(den[:], den[:], es[:], ALU.add))
                own.do(V.reciprocal(rden[:], den[:]))
                for b in range(NT):
                    lo, hi = a_keys(b) if kind == 0 else (0, 2 * P)
                    ins = V.tensor_scalar(prob[:, b, lo:hi], prob[:, b, lo:hi], rden[:, b:b + 1], None, ALU.mult)
                    ins.then_inc(s_p, 1)

            def k_norm(kv):
                dve.wait_ge(s_rks, kv + 1)
                own.do(V.reciprocal(rk[:], rk[:]))
                V.tensor_tensor(kn[:], kn[:], rk[:], ALU.mult).then_inc(s_kn, 1)

            def k_split(kv, kind):
                dve.wait_ge(s_khi, kv + 1)
                V.tensor_tensor(tokens(k_lo, kind), grid(kn[:], kind), tokens(k_hi, kind).bitcast(F32),
                                ALU.subtract).then_inc(s_klo, 1)

            def v_split(kv, src):
                dve.wait_ge(s_vhi, kv + 1)
                n = src.shape[1]
                V.tensor_tensor(v_lo[:, 0:n // P, :].rearrange("p a b -> p (a b)"), src,
                                v_hi[:, 0:n // P, :].rearrange("p a b -> p (a b)").bitcast(F32),
                                ALU.subtract).then_inc(s_vlo, 1)

            def pt_split(hh, kind):
                dve.wait_ge(s_pthi, hh + 1)
                hi = pt_hi[:].bitcast(F32)
                if kind == 0:
                    V.tensor_tensor(pt_lo[:, 0, P:3 * P], PS[:, 2, P:3 * P], hi[:, 0, P:3 * P], ALU.subtract)
                    V.tensor_tensor(pt_lo[:, 3, 0:2 * P], PS[:, 5, 0:2 * P], hi[:, 3, 0:2 * P], ALU.subtract)
                    V.tensor_tensor(pt_lo[:, 1:3, :], PS[:, 3:5, 0:3 * P], hi[:, 1:3, :],
                                    ALU.subtract).then_inc(s_ptlo, 1)
                else:
                    V.tensor_tensor(pt_lo[:, :, 0:2 * P], PS[:, 4:6, :].rearrange("p a (b c) -> p (a b) c", b=2),
                                    hi[:, :, 0:2 * P], ALU.subtract).then_inc(s_ptlo, 1)

            def o_split(hh, kind):
                dve.wait_ge(s_ohi, hh + 1)
                V.tensor_tensor(o_view(o_lo, hh, kind), o_psum(kind), o_view(o_hi, hh, kind).bitcast(F32),
                                ALU.subtract).then_inc(s_olo, 1)

            split(0, 0)
            for g in range(A_KV):
                for s in range(12):
                    split(12 * g + s + 1, 12 * g + s + 1)
                    last = A_GROUP * g - 1
                    if s == 0 and g:
                        q_tile(last, 1, 0)
                        pt_split(last - 1, 0)
                    if s == 1 and g:
                        o_split(last - 1, 0)
                        softmax(last, 0, sink[:, last:last + 1])
                        normalise(last, 0)
                    if s == 2 and g:
                        pt_split(last, 0)
                    if s == 3:
                        if g:
                            o_split(last, 0)
                        k_norm(g)
                    if s == 4:
                        k_split(g, 0)
                    if s == 5:
                        v_split(g, PS[:, 7, :])
                    if s >= 6 and s % 2 == 0:
                        a = (s - 6) // 2
                        q_tile(A_GROUP * g + a, a % 2, 0)
                        if a:
                            pt_split(A_GROUP * g + a - 1, 0)
                    if s >= 7 and s % 2 == 1:
                        a = (s - 7) // 2
                        hh = A_GROUP * g + a
                        if a:
                            o_split(hh - 1, 0)
                        softmax(hh, 0, sink[:, hh:hh + 1])
                        normalise(hh, 0)

            VB = PS[:, 4:6, :].rearrange("p a b -> p (a b)")

            def b_steps(h_, first):
                hh, kv, c0 = h_ + A_HEADS, h_ + A_KV, h_ * 6 + CH_B
                for s in range(6):
                    split(c0 + (s + 1), CH_B + s + 1)
                    if s == 0:
                        if first:
                            q_tile(A_HEADS - 1, 1, 0)
                            pt_split(A_HEADS - 2, 0)
                        else:
                            k_split(kv - 1, 1)
                    if s == 1:
                        if first:
                            o_split(A_HEADS - 2, 0)
                            softmax(A_HEADS - 1, 0, sink[:, A_HEADS - 1:A_HEADS])
                            normalise(A_HEADS - 1, 0)
                        else:
                            v_split(kv - 1, VB)
                            softmax(hh - 1, 1, None)
                            normalise(hh - 1, 1)
                    if s == 2:
                        q_tile(hh, 0, 1)
                        pt_split(hh - 1, 0 if first else 1)
                    if s == 3:
                        o_split(hh - 1, 0 if first else 1)
                    if s == 5:
                        k_norm(kv)

            b_steps(0, True)
            with dve.Fori(1, B_HEADS) as h_:
                own.loop(h_, 1, 10)
                b_steps(h_, False)
            own.done(B_HEADS - 1)

            def merge_b(j):
                dve.wait_ge(s_sgb, j + 1)
                dve.wait_ge(s_ta, j + 1)
                dve.wait_ge(s_chunk, j * 6 + (CH_M + 6))
                own.do(V.tensor_tensor(sig_b[:], sig_b[:], PS[:, 6, :], ALU.mult))
                out_ap = m_raw[:, j, :] if isinstance(j, int) else m_raw[:, ds(j, 1), :].rearrange("p o c -> p (o c)")
                V.tensor_tensor(out_ap, t_a[:], sig_b[:], ALU.add).then_inc(s_mg, 1)

            def m_steps(j, first):
                hh, kv = HEADS, A_KV + B_HEADS
                c0 = j * 6 + CH_M
                for s in range(6):
                    split(c0 + (s + 1), CH_M + s + 1)
                    if s == 0:
                        if first:
                            k_split(kv - 1, 1)
                        else:
                            merge_b(j - 1)
                    if first and s == 1:
                        v_split(kv - 1, VB)
                        softmax(hh - 1, 1, None)
                        normalise(hh - 1, 1)
                    if first and s == 2:
                        pt_split(hh - 1, 1)
                    if first and s == 3:
                        o_split(hh - 1, 1)
                    if s == 3:
                        dve.wait_ge(s_sga, j + 1)
                        dve.wait_ge(s_chunk, c0 + 3)
                        V.tensor_tensor(t_a[:], sig_a[:], PS[:, 1, :], ALU.mult).then_inc(s_ta, 1)

            m_steps(0, True)
            with dve.Fori(1, KT) as j:
                own.loop(j, 1, 1)
                m_steps(j, False)
            own.done(KT - 1)

            def merged_split(j):
                dve.wait_ge(s_mhi, j + 1)
                V.tensor_tensor(m_lo[:, j, :], m_raw[:, j, :], m_hi[:, j, :].bitcast(F32), ALU.subtract).then_inc(s_mlo, 1)

            merged_split(0)
            merged_split(1)
            merge_b(KT - 1)

            def h_add(nn):
                dve.wait_ge(s_xres, 32 * (nn + 1))
                dve.wait_ge(s_chunk, CH_O + 8 * nn + 8)
                for t in range(NT):
                    hv = h[:, t, nn * S:nn * S + S]
                    V.tensor_tensor(hv, PS[:, t, :], x_part(t), ALU.add).then_inc(s_h, 1)

            def x_part(t):
                return x_res[:, t, :] if t < 3 else x_last[:]

            for nn in range(NT):
                for c in range(8):
                    n = CH_O + 8 * nn + c
                    if nn and c == 0:
                        h_add(nn - 1)
                    if n + 1 < CH_END:
                        split(n + 1, n + 1)
                    if nn == 0 and c < 7:
                        merged_split(2 * c + 2)
                        merged_split(2 * c + 3)
                    if nn == 0 and c == 7:
                        dve.wait_ge(s_wr, 32)
                        dve.wait_ge(s_wrg, 16 * 5)
                        V.tensor_tensor(wr[:], wr[:], bc(g2c[:], LOG), ALU.mult).then_inc(s_dve2, 1)
            h_add(NT - 1)
            routing(dve, own, V)
            dve.wait_ge(s_r1, 1)
            items = dve.value_load(nitem[0:1, 0:1], min_val=EXPERTS, max_val=EXPERTS + XTRA)
            g2b = bc(g2m[:], SLOTS)

            def x_copy(i):
                dve.wait_ge(s_xt2, i + 1)
                V.tensor_tensor(xT[:], PS[:, 2:4, :].rearrange("p a (k s) -> p (a k) s", s=SLOTS), g2b,
                                ALU.mult).then_inc(s_xTc, 1)

            def add_parts(i):
                for r in range(8):
                    t, m, bank = r // 2, r % 2, (2, 6)[r % 2]
                    dve.wait_ge(s_comb, i * 8 + (r + 1))
                    hv = h[:, t, :].rearrange("p (f m c) -> p m f c", f=2, m=2)[:, m]
                    V.tensor_tensor(hv, hv, PS[:, bank:bank + 2, :], ALU.add).then_inc(s_added, 1)

            V.tensor_scalar(y_hi[:].rearrange("p (a b) -> p a b", a=2), rep(token[:], 2), 0.0, None, ALU.mult)
            V.tensor_scalar(y_lo[:].rearrange("p (a b) -> p a b", a=2), rep(token[:], 2), 0.0, None, ALU.mult)
            V.tensor_scalar(place[:], token[:], 0.0, None, ALU.mult).then_inc(s_ylo, 1)
            dve.sem_inc(s_added, 2)
            dve.wait_ge(s_hd, 16 * NT)
            x_copy(0)
            with dve.Fori(0, items) as i:
                own.loop(i, 0, 2)
                add_parts(i)
                dve.wait_ge(s_sgm, i + 1)
                own.do(V.tensor_tensor(t1[:], sg[:], PS[:, 0, 0:F // 2], ALU.mult))
                V.tensor_tensor(hs[:], t1[:], PS[:, 1, 0:F // 2], ALU.mult).then_inc(s_hs, 1)
                dve.wait_ge(s_hst, i + 1)
                V.tensor_copy(hT[:], PS[:, 6, 0:2 * P].rearrange("p (c s) -> p c s", c=2)).then_inc(s_hTc, 1)
                x_copy(i + 1)
                own.do(V.tensor_copy(cur[:], tab[:, 0:2, ds(i, 1)].rearrange("p c o -> p (c o)")))
                V.tensor_scalar(place[:], token[:], cur[:, 0:1], None, ALU.is_equal)
                dve.wait_ge(s_yhi, i + 1)
                V.scalar_tensor_tensor(out=y_lo[:], in0=PS[:, 4:6, :].rearrange("p a b -> p (a b)"), scalar=cur[:, 1:2],
                                       in1=y_hi[:].bitcast(F32), op0=ALU.mult, op1=ALU.subtract).then_inc(s_ylo, 1)
            add_parts(items)

        @block.tensor
        def _(pe):
            mm = nc.tensor.matmul
            pe.wait_ge(s_const, 16)
            for G in range(16):
                t, kk = G // 4, G % 4
                if kk == 0:
                    pe.wait_ge(s_xn, t + 1)
                if G >= 8:
                    pe.wait_ge(s_xlo, G - 7)
                for q in range(4):
                    k = 4 * kk + q
                    last = nc.tensor.transpose(PS[:, G % 8, q * P:q * P + P], xt[:, t, k * P:k * P + P], ident)
                last.then_inc(s_xtr, 1)
            pe.wait_ge(s_oh, 48)
            pe.wait_ge(s_xlo, 16)
            mm(PS[0:A_HEADS, 7, :], small["table"][0:BUCKETS, :], onehot[:], start=True, stop=True).then_inc(s_pos, 1)

            def chunk(n, python_n, bank, rhs_hi, rhs_lo, k0, start, stop, transposed=None):
                pe.wait_ge(s_wlo, n + 1)
                wh = w_hi[:, python_n % SPLIT, :].rearrange("p (k c) -> p k c", k=8)
                wl = w_lo[:, python_n % SPLIT, :].rearrange("p (k c) -> p k c", k=8)
                for k in range(8):
                    if k == 4 and transposed:
                        p_transpose(*transposed)
                    mm(PS[:, bank, :], wh[:, k, :], rhs_hi[:, k0 + k, :], start=(start and k == 0), stop=False)
                    mm(PS[:, bank, :], wh[:, k, :], rhs_lo[:, k0 + k, :], start=False, stop=False)
                    last = mm(PS[:, bank, :], wl[:, k, :], rhs_hi[:, k0 + k, :], start=False, stop=(stop and k == 7))
                last.then_inc(s_chunk, 1)

            def q_sums(hh, bank, kind):
                pe.wait_ge(s_sqq, hh + 1)
                for t in range(NT):
                    last = mm(PS[:, bank, t:t + 1], sq[:, t * P:t * P + P], ones[:, 0:1], start=True, stop=True)
                last.then_inc(s_qsum, 1)

            def k_sums(kv, bank):
                pe.wait_ge(s_sqk, kv + 1)
                mm(PS[:, bank, :], ones, sq[:], start=True, stop=True).then_inc(s_ksum, 1)

            def three(o, a_hi, a_lo, b_hi, b_lo, start=True, stop=True):
                mm(o, a_hi, b_hi, start=start, stop=False)
                mm(o, a_lo, b_hi, start=False, stop=False)
                return mm(o, a_hi, b_lo, start=False, stop=stop)

            def scores(hh, kind, kv):
                pe.wait_ge(s_qlo, hh + 1)
                pe.wait_ge(s_klo, kv + 1)
                for b in range(NT):
                    if kind == 0:
                        lo, hi = a_keys(b)
                        k0 = (b - 1) * P
                        qs = [q[:, b * P:b * P + P] for q in (q_hi, q_lo)]
                        ks = [k[:, k0 + lo:k0 + hi] for k in (k_hi, k_lo)]
                        o = PS[:, 2 + b, lo:hi]
                    else:
                        k0 = B_START[b] * ROWS
                        qs = [q[:, b * P:b * P + P] for q in (q_hi, q_lo)]
                        ks = [k[:, k0:k0 + 2 * P] for k in (k_hi, k_lo)]
                        o = PS[:, 2 + b // 2, (b % 2) * 256:(b % 2) * 256 + 256]
                    last = three(o, *qs, *ks)
                last.then_inc(s_sc, 1)

            def v_transpose(kv, kind):
                pe.wait_ge(s_vt, kv + 1)
                if kind == 0:
                    for t in range(NT):
                        last = nc.tensor.transpose(PS[:, 7, t * P:t * P + P], vt[:, t * P:t * P + P], ident)
                else:
                    for b in range(NT):
                        for kt in range(2):
                            c = (b % 2) * 256 + kt * P
                            last = nc.tensor.transpose(PS[:, 4 + b // 2, c:c + P],
                                                       vt[:, B_START[b] * ROWS + kt * P:B_START[b] * ROWS + kt * P + P],
                                                       ident)
                last.then_inc(s_vtr, 1)

            def p_transpose(hh, kind):
                for b in range(NT):
                    pe.wait_ge(s_p, hh * 4 + (b + 1))
                    lo, hi = a_keys(b) if kind == 0 else (0, 2 * P)
                    for c in range(lo, hi, P):
                        if kind == 0:
                            o = PS[:, 2 + b, c:c + P]
                        else:
                            o = PS[:, 4 + b // 2, (b % 2) * 256 + c:(b % 2) * 256 + c + P]
                        last = nc.tensor.transpose(o, prob[:, b, c:c + P], ident)
                last.then_inc(s_ptr, 1)

            def pv(hh, kind, kv):
                pe.wait_ge(s_ptlo, hh + 1)
                pe.wait_ge(s_vlo, kv + 1)
                for b in range(NT):
                    lo, hi = a_keys(b) if kind == 0 else (0, 2 * P)
                    for c in range(lo, hi, P):
                        vi = (b - 1 + c // P) if kind == 0 else (2 * b + c // P)
                        last = three(PS[:, 6, b * P:b * P + P], v_hi[:, vi, :], v_lo[:, vi, :], pt_hi[:, b, c:c + P],
                                     pt_lo[:, b, c:c + P], start=(c == lo), stop=(c + P >= hi))
                last.then_inc(s_pv, 1)

            for g in range(A_KV):
                for s in range(12):
                    n, tile = 12 * g + s, s // 2
                    hh0 = A_GROUP * g
                    if s % 2 == 0:
                        if tile == 0 and g:
                            pe.wait_ge(s_qlo, hh0 - 1)
                            pe.wait_ge(s_sqq, hh0 - 1)
                        elif tile == 1 and g:
                            pe.wait_ge(s_qlo, hh0)
                            pe.wait_ge(s_sqq, hh0)
                        elif tile == 2:
                            pe.wait_ge(s_sqk, g + 1)
                        elif tile == 3:
                            pe.wait_ge(s_vt, g + 1)
                        elif tile > 3:
                            pe.wait_ge(s_qlo, hh0 + tile - 3)
                            pe.wait_ge(s_sqq, hh0 + tile - 3)
                    if n == 0:
                        pe.wait_ge(s_xlo, 16)
                    if s == 0:
                        transposed = (hh0 - 2, 0) if g else None
                    elif s == 2:
                        transposed = (hh0 - 1, 0) if g else None
                    else:
                        transposed = (hh0 + (s - 8) // 2, 0) if s >= 8 and s % 2 == 0 else None
                    chunk(n, n, tile % 2, x_hi, x_lo, 8 * (s % 2), s % 2 == 0, s % 2 == 1, transposed)
                    if s == 0 and g:
                        pe.wait_ge(s_olo, hh0 - 2)
                        pv(hh0 - 2, 0, g - 1)
                        pe.wait_ge(s_rqs, hh0 - 1)
                        q_sums(hh0 - 1, 7, 0)
                        scores(hh0 - 1, 0, g - 1)
                    if s == 2:
                        if g:
                            pe.wait_ge(s_olo, hh0 - 1)
                            pv(hh0 - 1, 0, g - 1)
                            pe.wait_ge(s_rqs, hh0)
                        else:
                            pe.wait_ge(s_tv, 1)
                        k_sums(g, 7)
                    if s == 4:
                        pe.wait_ge(s_rks, g + 1)
                        v_transpose(g, 0)
                    if s >= 6 and s % 2 == 0:
                        hh = hh0 + (s - 6) // 2
                        if hh > hh0:
                            if hh > 1:
                                pe.wait_ge(s_olo, hh - 1)
                            pv(hh - 1, 0, g)
                            pe.wait_ge(s_rqs, hh)
                        else:
                            pe.wait_ge(s_vlo, g + 1)
                        q_sums(hh, 7, 0)
                        scores(hh, 0, g)

            def b_steps(h_, first):
                hh, kv, c0 = h_ + A_HEADS, h_ + A_KV, h_ * 6 + CH_B
                pk = 0 if first else 1
                for s in range(6):
                    if s == 0:
                        pe.wait_ge(s_qlo, hh - 1 if first else hh)
                        pe.wait_ge(s_sqq, hh - 1 if first else hh)
                    if s == 2:
                        pe.wait_ge(s_qlo, hh)
                        pe.wait_ge(s_sqq, hh)
                        pe.wait_ge(s_sqk, kv)
                    if s == 4:
                        if first:
                            pe.wait_ge(s_rqs, hh)
                        else:
                            pe.wait_ge(s_vt, kv)
                    if s == 0:
                        transposed = (A_HEADS - 2, 0) if first else None
                    elif s == 2:
                        if not first:
                            pe.wait_ge(s_vlo, kv)
                        transposed = (hh - 1, pk)
                    else:
                        transposed = None
                    chunk(c0 + s, CH_B + s, (0, 1, 7)[s // 2], x_hi, x_lo, 8 * (s % 2), s % 2 == 0, s % 2 == 1,
                          transposed)
                    if s == 0:
                        if first:
                            pe.wait_ge(s_olo, A_HEADS - 2)
                            pv(A_HEADS - 2, 0, A_KV - 1)
                            pe.wait_ge(s_rqs, A_HEADS - 1)
                            q_sums(A_HEADS - 1, 7, 0)
                            scores(A_HEADS - 1, 0, A_KV - 1)
                        else:
                            pe.wait_ge(s_rqs, hh)
                            v_transpose(kv - 1, 1)
                            scores(hh - 1, 1, kv - 1)
                    if s == 2:
                        pe.wait_ge(s_rks, kv)
                        pe.wait_ge(s_olo, hh - 1)
                        pv(hh - 1, pk, kv - 1)
                        q_sums(hh, 4, 1)
                    if s == 4:
                        pe.wait_ge(s_olo, hh)
                        k_sums(kv, 6)

            b_steps(0, True)
            with pe.Fori(1, B_HEADS) as h_:
                b_steps(h_, False)

            def m_steps(j, first):
                hh, kv, c0 = HEADS, A_KV + B_HEADS, j * 6 + CH_M
                for s in range(6):
                    if s == 0:
                        if first:
                            pe.wait_ge(s_sqq, hh)
                            pe.wait_ge(s_qlo, hh)
                        else:
                            pe.wait_ge(s_sga, j)
                    if s == 2:
                        if first:
                            pe.wait_ge(s_sqk, kv)
                        else:
                            pe.wait_ge(s_ta, j)
                    if s == 3:
                        if first:
                            pe.wait_ge(s_vt, kv)
                        else:
                            pe.wait_ge(s_sgb, j)
                    if s == 5:
                        if first:
                            pe.wait_ge(s_olo, hh)
                        else:
                            pe.wait_ge(s_mg, j)
                    n = c0 + s
                    pn = CH_M + s
                    if s < 2:
                        chunk(n, pn, 0, x_hi, x_lo, 8 * s, s == 0, s == 1)
                    elif s == 2:
                        if first:
                            pe.wait_ge(s_vlo, kv)
                        chunk(n, pn, 1, o_hi, o_lo, 0, True, True, (hh - 1, 1) if first else None)
                    elif s < 5:
                        chunk(n, pn, 7, x_hi, x_lo, 8 * (s - 3), s == 3, s == 4)
                    else:
                        chunk(n, pn, 6, o_hi, o_lo, A_HEADS, True, True)
                    if first and s == 0:
                        pe.wait_ge(s_rqs, hh)
                        v_transpose(kv - 1, 1)
                        scores(hh - 1, 1, kv - 1)
                    if first and s == 2:
                        pe.wait_ge(s_rks, kv)
                        pe.wait_ge(s_olo, hh - 1)
                        pv(hh - 1, 1, kv - 1)

            m_steps(0, True)
            with pe.Fori(1, KT) as j:
                m_steps(j, False)

            def h_transpose(k):
                pe.wait_ge(s_h, 4 * (k // 4) + 4)
                if k >= 2:
                    pe.wait_ge(s_htc, k - 1)
                for t in range(NT):
                    last = nc.tensor.transpose(PS[:, 4 + k % 2, t * P:t * P + P], h[:, t, k * P:k * P + P], ident)
                last.then_inc(s_htr, 1)

            def logits(k):
                pe.wait_ge(s_htc, k + 1)
                mm(PS[0:LOG, 7, :], wr[:, k, :], h_t[:], start=(k == 0), stop=(k == 4 * NT - 1)).then_inc(s_lg, 1)

            pe.wait_ge(s_sga, KT)
            pe.wait_ge(s_ta, KT)
            for nn in range(NT):
                for c in range(8):
                    n = CH_O + 8 * nn + c
                    pe.wait_ge(s_wlo, n + 1)
                    wh = w_hi[:, n % SPLIT, :].rearrange("p (k c) -> p k c", k=2)
                    wl = w_lo[:, n % SPLIT, :].rearrange("p (k c) -> p k c", k=2)
                    if nn == 0:
                        pe.wait_ge(s_mlo, 2 * c + 2)
                    for kk in range(2):
                        k = 2 * c + kk
                        for t in range(NT):
                            if k == 0 and nn:
                                pe.wait_ge(s_h, 4 * (nn - 1) + t + 1)
                            a, b = m_hi[:, k, t * P:t * P + P], m_lo[:, k, t * P:t * P + P]
                            last = three(PS[:, t, :], a, b, wh[:, kk, :], wl[:, kk, :], start=(k == 0), stop=(k == KT - 1))
                    last.then_inc(s_chunk, 1)
                    if nn and 1 <= c < 5:
                        h_transpose(4 * (nn - 1) + c - 1)
                    if nn and 2 <= c < 6:
                        if c == 2 and nn == 1:
                            pe.wait_ge(s_dve2, 1)
                        logits(4 * (nn - 1) + c - 2)
            k0 = 4 * NT - 4
            h_transpose(k0)
            for k in range(k0, 4 * NT):
                if k + 1 < 4 * NT:
                    h_transpose(k + 1)
                logits(k)
            pe.wait_ge(s_lgc, 1)
            pe.wait_ge(s_htc, 4 * NT)
            for t in range(NT):
                last = nc.tensor.transpose(PS[:, 0, t * LOG:t * LOG + LOG], rt["lgT"][:, t * P:t * P + P],
                                           mats[0:LOG, 0, 0:LOG])
            last.then_inc(s_lgT, 1)
            pe.wait_ge(s_M, 4)
            Ms = rt["Ms"]
            for t in range(NT):
                for u in range(t):
                    mm(PS[:, 1, t * 32:t * 32 + 32], ones, Ms[:, u, :], start=(u == 0), stop=False)
                mm(PS[:, 1, t * 32:t * 32 + 32], upper, Ms[:, t, :], start=(t == 0), stop=True)
            for u in range(NT):
                last = mm(PS[:, 1, 128:160], ones, Ms[:, u, :], start=(u == 0), stop=(u == NT - 1))
            last.then_inc(s_pos, 1)
            pe.wait_ge(s_ent, 1)
            for j in range(8):
                last = mm(PS[:, 0, 0:3 * ITEMS], rt["slot1h"][:, j, :], rt["entries"][:, j, :, :].rearrange("p c i -> p (c i)"),
                          start=(j == 0), stop=(j == 7))
            last.then_inc(s_tab, 1)
            pe.wait_ge(s_r1, 1)
            items = pe.value_load(nitem[0:1, 0:1], min_val=EXPERTS, max_val=EXPERTS + XTRA)
            pe.wait_ge(s_nreg, 1)

            def x_transpose(i):
                pe.wait_ge(s_xs, i + 1)
                settle(pe, s_pe_passed)
                v = xg[:].rearrange("s (p k) -> s k p", k=KT)
                for k in range(KT):
                    o = PS[:, 2 + k // 8, (k % 8) * SLOTS:(k % 8) * SLOTS + SLOTS]
                    last = nc.tensor.transpose(o, v[:, k, :], mats[0:SLOTS, 0, 0:SLOTS])
                last.then_inc(s_xt2, 1)

            def combine(i, c):
                for r in (2 * c, 2 * c + 1):
                    t, m, bank = r // 2, r % 2, (2, 6)[r % 2]
                    pe.wait_ge(s_added, i * 8 + (r + 1))
                    for y in (y_hi, y_lo):
                        for f in range(2):
                            last = mm(PS[:, bank + f, :], place[SLOTS * f:SLOTS * f + SLOTS, t * P:t * P + P],
                                      y[SLOTS * f:SLOTS * f + SLOTS, m * S:m * S + S], start=(y is y_hi), stop=(y is y_lo))
                    last.then_inc(s_comb, 1)

            x_transpose(0)
            with pe.Fori(0, items) as i:
                pe.wait_ge(s_xTc, i + 1)
                for c in range(4):
                    pe.wait_ge(s_wg[c], i * 16 + 16)
                    pe.wait_ge(s_wu[c], i * 16 + 16)
                    for k in range(4 * c, 4 * c + 4):
                        for bank, w in ((0, wg_s), (1, wu_s)):
                            for f in range(2):
                                last = mm(PS[SLOTS * f:SLOTS * f + SLOTS, bank, 0:F // 2], xT[:, k, :],
                                          w[:, k, f * (F // 2):(f + 1) * (F // 2)], start=(k == 0), stop=(k == KT - 1))
                    last.then_inc(s_gu, 1)
                    if c == 0:
                        pe.wait_ge(s_ylo, i + 1)
                    combine(i, c)
                pe.wait_ge(s_added, i * 8 + 9)
                x_transpose(i + 1)
                pe.wait_ge(s_added, i * 8 + 10)
                pe.wait_ge(s_hs, i + 1)
                hv = hs[:].rearrange("p (f c) -> p c f", c=2)
                for c in range(2):
                    last = nc.tensor.transpose(PS[:, 6, c * P:c * P + P], hv[:, c, :], ident)
                last.then_inc(s_hst, 1)
                pe.wait_ge(s_hTc, i + 1)
                for c in range(4):
                    j, cc = c // 2, c % 2
                    pe.wait_ge(s_wd[c], i * 16 + 16)
                    for m in range(2):
                        for f in range(2):
                            last = mm(PS[SLOTS * f:SLOTS * f + SLOTS, 4 + m, :], hT[:, cc, SLOTS * j:SLOTS * j + SLOTS],
                                      wd_s[:, c, f * (D // 2) + m * S:f * (D // 2) + m * S + S],
                                      start=(c == 0), stop=(c == 3))
                    last.then_inc(s_dn, 1)
            pe.wait_ge(s_ylo, items + 1)
            for c in range(NT):
                combine(items, c)


_INS = ['x', 'norm1_g', 'w_in', 'q_norm_a', 'k_norm_a', 'sink_a', 'q_norm_b', 'k_norm_b', 'rpb_b', 'w_up_a',
        'w_up_b', 'w_out', 'rel_bias_table', 'norm2_g', 'w_router_group', 'b_router_group',
        'w_router_expert', 'b_router_expert', 'w_gate', 'w_up', 'w_down']


def constants():
    f = np.float32
    i = np.arange(P)
    mats = np.stack([np.eye(P, dtype=f), np.ones((P, P), f), np.triu(np.ones((P, P), f), 1)], axis=1)
    rel = np.arange(S) - (2 * WINDOW - 1)
    half_b = BUCKETS // 2
    exact = half_b // 2
    n = np.abs(rel)
    nf = np.maximum(n, 1).astype(f)
    large = exact + (np.log(nf / f(exact)) / f(np.log(MAXDIST / exact)) * f(half_b - exact)).astype(np.int32)
    bucket = np.where(rel > 0, half_b, 0) + np.where(n < exact, n, np.minimum(large, half_b - 1))
    onehot = (bucket[None, :] == np.arange(BUCKETS)[:, None]).astype(f)
    mask_a = np.broadcast_to(np.where(n <= WINDOW, 0.0, NEG).astype(f), (A_HEADS, S))
    mask_b = np.zeros((P, 3, ROWS, KC), f)
    for b in range(NT):
        qc = QC * b + i // ROWS
        kc = B_START[b] + np.arange(KC)
        w0 = np.clip(qc - NB_COLS // 2, 0, GRID_W - NB_COLS)[:, None]
        ok = (kc[None, :] >= w0) & (kc[None, :] < w0 + NB_COLS)
        mask_b[:, B_KIND[b]] = np.where(ok, 0.0, NEG).astype(f)[:, None, :]
    ramp = np.zeros((P, 160 + SLOTS), f)
    ramp[:, 0:16] = np.tile([4, 3, 2, 1], 4)
    ramp[:, 32:160] = np.tile(np.arange(32, 0, -1), 4)
    ramp[:, 160:] = np.arange(SLOTS)
    entry = np.zeros((P, 3, 2, NT), f)
    entry[:, 0] = (i[:, None] + P * np.arange(NT)[None, :] - 2 * S)[:, None, :]
    tokens = np.broadcast_to(np.arange(S, dtype=f), (P, S))
    c = np.ascontiguousarray
    return {"c_mats": c(mats), "c_onehot": onehot, "c_maska": c(mask_a), "c_maskb": c(mask_b.reshape(P, 3, 2 * P)),
            "c_ramp": ramp, "c_entry": c(entry.reshape(P, 24)), "c_tokens": c(tokens)}


def kernel(**inputs):
    from concourse import bacc
    from concourse.bass_utils import run_bass_kernel_spmd as run

    nc = bacc.Bacc("TRN2", target_bir_lowering=False, num_devices=1)
    arrays, args = {}, []
    feed = [(n, np.ascontiguousarray(inputs[n])) for n in _INS]
    rpb = feed[8][1][0]
    pad = np.zeros((B_HEADS, 2 * NB_ROWS - 1, RPB_W), rpb.dtype)
    pad[:, :, NB_COLS:NB_COLS + 2 * NB_COLS - 1] = rpb
    feed[8] = ("rpb_pad", pad)
    feed += list(constants().items())
    for name, a in feed:
        arrays[f"in_{name}"] = a
        args.append(nc.dram_tensor(f"in_{name}", a.shape, mybir.dt.from_np(a.dtype), kind="ExternalInput").ap())
    for name, shape in (("tvec", [A_HEADS, S]), ("h", [S, D]), ("wide", [B_HEADS, P, ROWS * 3 * QC]), ("bias", [A_HEADS, P, 3 * P])):
        args.append(nc.dram_tensor(f"{name}_dram", shape, F32, kind="Internal").ap())
    args.append(nc.dram_tensor("out_0", [1, S, D], F32, kind="ExternalOutput").ap())
    build(nc, *args)
    r = run(nc, [arrays], core_ids=[0])
    return r.results[0]["out_0"]
```

```python
from contextlib import ExitStack

import numpy as np
import concourse.bass as bass
from concourse import mybir

F32 = mybir.dt.float32
F32R = mybir.dt.float32r
U32 = mybir.dt.uint32
I32 = mybir.dt.int32
ALU = mybir.AluOpType
ACT = mybir.ActivationFunctionType
AX = mybir.AxisListType.X
ds = bass.ds

P = 128
D = 2048
S = 512
KT = D // P
NT = S // P
HD = 128
A_HEADS, A_KV, A_GROUP = 8, 2, 4
B_HEADS = 8
HEADS = A_HEADS + B_HEADS
BUCKETS, WINDOW, MAXDIST = 32, 128, 128
GRID_W, ROWS = 64, S // 64
NB_ROWS, NB_COLS = 8, 16
QC = GRID_W // NT
KC = 2 * QC
B_START = [min(max(QC * b - NB_COLS // 2, 0), GRID_W - KC) for b in range(NT)]
B_KIND = [(QC * b - B_START[b]) // 8 for b in range(NT)]
A_WIDTH, A_KVW, B_WIDTH = A_HEADS * HD, A_KV * HD, B_HEADS * HD
COL_QA = 0
COL_KA = A_WIDTH
COL_VA = COL_KA + A_KVW
COL_QB = COL_VA + A_KVW
COL_KB = COL_QB + B_WIDTH
COL_VB = COL_KB + B_WIDTH
COL_GA = COL_VB + B_WIDTH
COL_GB = COL_GA + D
GROUPS, PER_GROUP, EXPERTS, F = 4, 8, 32, 512
LOG = GROUPS + EXPERTS
EPS = 1e-6
NEG = -1e30
SLOTS = 64
MORE = S // SLOTS - 1
XTRA = 2 * S // SLOTS
ITEMS = EXPERTS + XTRA + 1
RPB_W = 2 * NB_COLS - 1 + 2 * NB_COLS
RAW, SPLIT = 3, 2
CH_A = 0
CH_B = CH_A + 2 * (A_KV * 2 + A_HEADS)
CH_M = CH_B + 6 * B_HEADS
CH_O = CH_M + 6 * KT
CH_END = CH_O + NT * 8


def a_keys(b):
    return (P if b == 0 else 0), (2 * P if b == NT - 1 else 3 * P)


class Chain:

    def __init__(self, eng, sem):
        self.eng, self.sem, self.base, self.n = eng, sem, 0, 0

    def link(self, ins):
        self.n += 1
        ins.then_inc(self.sem, 1)
        return ins

    def wait(self, back=0):
        self.eng.wait_ge(self.sem, self.base + (self.n - back))

    def do(self, ins):
        self.link(ins)
        self.wait()

    def loop(self, i, first, per):
        self.start, self.per, self.rounds = self.base + self.n, per, None
        self.base, self.n = (i - first) * per + self.start, 0

    def done(self, rounds):
        assert self.n == self.per, (self.n, self.per)
        self.base, self.n = 0, self.start + rounds * self.per


def bc(ap, n):
    return bass.AP(ap.tensor, ap.offset, [list(x) for x in ap.ap] + [[0, n]])


def wide_of(ap, n):
    return bass.AP(ap.tensor, ap.offset, [list(ap.ap[0]), [0, n]])


def rep(ap, n):
    a = [list(x) for x in ap.ap]
    return bass.AP(ap.tensor, ap.offset, a[:1] + [[0, n]] + a[1:])


def build(nc, x, norm1_g, w_in, q_norm_a, k_norm_a, sink_a, q_norm_b, k_norm_b, rpb_pad, w_up_a, w_up_b,
          w_out, rel_bias_table, norm2_g, w_router_group, b_router_group, w_router_expert,
          b_router_expert, w_gate, w_up, w_down, c_mats, c_onehot, c_maska, c_maskb, c_ramp, c_entry,
          c_tokens, tvec_d, h_d, wide_d, bias_d, out):
    ctx = ExitStack()
    with ctx:
        at = [0]

        def sb(name, shape, dt, offset):
            size = 4 * int(np.prod(shape[1:]))
            at[0] = offset + size
            return nc.alloc_sbuf_tensor_at(name, shape, dt, offset=offset)

        def sem(name):
            return ctx.enter_context(nc.semaphore(name))

        K = 1024
        base = -(-nc.sbuf_base // 32) * 32
        R0, R1, R2, R3, R4 = (base + n * K for n in (0, 64, 128, 160, 198))
        x_hi = sb("x_hi", [P, KT, S], F32R, R0)
        x_lo = sb("x_lo", [P, KT, S], F32R, R0 + 32 * K)
        m_hi = sb("m_hi", [P, KT, S], F32R, R0)
        m_lo = sb("m_lo", [P, KT, S], F32R, R0 + 32 * K)
        wd_s = sb("wd_s", [P, 4, D], F32, R0)
        xg = sb("xg", [SLOTS, D], F32, R0 + 32 * K)
        xT = sb("xT", [P, KT, SLOTS], F32, R0 + 40 * K)
        y_hi = [sb(f"y_hi{f}", [P, D // 2], F32R, (R0 + 44 * K, R3 + 32 * K)[f]) for f in range(2)]
        y_lo = [sb(f"y_lo{f}", [P, D // 2], F32R, (R0 + 48 * K, R4 + 1536)[f]) for f in range(2)]
        place = [sb(f"place{f}", [P, S], F32R, (R0 + 56 * K, R3 + 36 * K)[f]) for f in range(2)]
        sg = sb("sg", [P, F // 2], F32, R0 + 52 * K)
        t1 = sb("t1", [P, F // 2], F32, R0 + 53 * K)
        hs = sb("hs", [P, F // 2], F32, R0 + 54 * K)
        hT = sb("hT", [P, 2, P], F32, R0 + 55 * K)
        token = sb("token", [P, S], F32, R0 + 62 * K)
        tab = sb("tab", [P, 3, ITEMS], F32, R0 + 60 * K)
        idx_x = sb("idx_x", [SLOTS, ITEMS], U32, R0 + 61 * K)
        cur_x = sb("cur_x", [SLOTS, 1], U32, R0 + 61 * K + 256)
        cur = sb("cur", [P, 2], F32, R0 + 61 * K + 288)
        eid = sb("eid", [P, XTRA], I32, R0 + 61 * K + 320)
        nitem = sb("nitem", [P, 3], I32, R0 + 61 * K + 384)
        xt = sb("xt", [P, NT, D], F32, R1)
        o_hi = sb("o_hi", [P, HEADS, S], F32R, R1)
        o_lo = sb("o_lo", [P, HEADS, S], F32R, R1 + 32 * K)
        h = sb("h", [P, NT, D], F32, R1)
        wg_s = sb("wg_s", [P, KT, F], F32, R1 + 32 * K)
        w_raw = sb("w_raw", [P, RAW, 8 * P], F32, R2)
        bias = sb("bias", [P, 3, 2 * P], F32, R2 + 12 * K)
        w_hi = sb("w_hi", [P, SPLIT, 8 * P], F32R, R2 + 16 * K)
        w_lo = sb("w_lo", [P, SPLIT, 8 * P], F32R, R2 + 24 * K)
        gb = sb("gb", [P, D], F32, R3)
        junk = sb("junk", [P, D], F32, R3 + 8 * K)
        v_t = sb("v_t", [P, 8, P], F32, R3)
        q_hi = sb("q_hi", [P, S], F32R, R3 + 8 * K)
        q_lo = sb("q_lo", [P, S], F32R, R3 + 10 * K)
        prob = sb("prob", [P, 4, 3 * P], F32, R3 + 12 * K)
        rk = sb("rk", [P, S], F32, R3 + 12 * K)
        p_t = sb("p_t", [P, 4, 3 * P], F32, R3 + 18 * K)
        kn = sb("kn", [P, S], F32, R3 + 30 * K)
        sq = sb("sq", [P, S], F32, R3 + 32 * K)
        vt = sb("vt", [P, S], F32, R3 + 32 * K)
        k_hi = sb("k_hi", [P, S], F32R, R3 + 34 * K)
        k_lo = sb("k_lo", [P, S], F32R, R3 + 36 * K)
        m_raw = sb("m_raw", [P, KT, S], F32, R3)
        sig_a = sb("sig_a", [P, S], F32, R3 + 32 * K)
        t_a = sb("t_a", [P, S], F32, R3 + 34 * K)
        sig_b = sb("sig_b", [P, S], F32, R3 + 36 * K)
        wu_s = sb("wu_s", [P, KT, F], F32, R3)
        x_res = sb("x_res", [P, 3, S], F32, R3 + 32 * K)
        x_last = sb("x_last", [P, S], F32, R2 + 12 * K)
        h_t2 = sb("h_t2", [P, S], F32, R2 + 14 * K)
        wg_odd = sb("wg_odd", [P, KT, F], F32, R2)
        o4 = R4
        mats = sb("mats", [P, 3, P], F32, o4)
        mask_b = sb("mask_b", [P, 3, 2 * P], F32, o4 + 1536)
        wr = sb("wr", [P, KT, LOG], F32, o4 + 1536)
        h_t = sb("h_t", [P, S], F32, o4 + 3840)
        o4 += 5888
        small = {}
        for name, n in (("gq", 2), ("gk", 2), ("g2c", KT), ("g2m", KT), ("sink", A_HEADS), ("eps", 2), ("ssx", 4), ("rsx", 4),
                        ("rx", 4), ("rqs", 4), ("rq", 4), ("mx", 4), ("negm", 4), ("den", 4), ("es", 4),
                        ("rden", 4), ("ssh", 16), ("ssum", 4), ("rh", 4), ("rb", LOG),
                        ("ramp4", 16), ("table", A_HEADS), ("rhs_", 4)):
            small[name] = sb(name, [P, n], F32, o4)
            o4 += -(-4 * n // 32) * 32
        wide = sb("wide", [P, ROWS, 3 * QC], F32, o4)
        rt_ent = sb("r_ent", [P, 3, 8], F32, o4)
        rt_ramp = sb("r_ramp", [P, 4, 32], F32, o4 + 96)
        rt_iota = sb("r_iota", [P, SLOTS], F32, o4 + 608)
        assert o4 + 4 * ROWS * 3 * QC <= nc.sbuf_usable_end, o4
        gq, gk, g2c, g2m, sink, eps = (small[n] for n in ("gq", "gk", "g2c", "g2m", "sink", "eps"))
        ssx, rsx, rx, rqs, rq, mx, negm = (small[n] for n in ("ssx", "rsx", "rx", "rqs", "rq", "mx", "negm"))
        den, es, rden, ssh, ssum, rh = (small[n] for n in ("den", "es", "rden", "ssh", "ssum", "rh"))
        rb, ramp4, rhs_ = small["rb"], small["ramp4"], small["rhs_"]
        ident, ones, upper = mats[:, 0, :], mats[:, 1, :], mats[:, 2, :]
        onehot = sb("onehot", [BUCKETS, S], F32, R3 + 16 * K)
        mask_a = sb("mask_a", [A_HEADS, S], F32, R3 + 18 * K)
        tvec = sb("tvec", [A_HEADS, S], F32, R3 + 20 * K)
        o2 = R0 + 40 * K
        rt = {"ent": rt_ent, "ramp": rt_ramp, "iota": rt_iota}
        for name, shape in (("L", [P, NT, LOG]), ("gm", [P, 4]), ("gd", [P, 4, 4]), ("eg", [P, 4, 4]),
                            ("sgm", [P, 4]), ("pg", [P, 4]), ("gs", [P, 4, 4]), ("gx", [P, 4]), ("oh", [P, 4, 4]),
                            ("pen", [P, 4, 4]), ("em", [P, 4, 32]), ("v1", [P, 4]),
                            ("s1", [P, 4, 32]), ("x1", [P, 4]), ("M12", [P, 2, 4, 32]), ("em2", [P, 4, 32]),
                            ("v2", [P, 4]), ("e2", [P, 4]), ("dn", [P, 4]), ("rr", [P, 4]), ("w12", [P, 2, 4]),
                            ("Ms", [P, 4, 32]), ("before", [P, 5, 32]), ("steps", [P, MORE]), ("over", [P, 32, MORE]), ("nb", [P, 48]),
                            ("xa", [P, 48]), ("xb", [P, 48]), ("xo", [P, 32]),
                            ("eidf", [P, XTRA]), ("pr", [P, 2, 4, 32]), ("pk", [P, 8]),
                            ("ek", [P, 8]), ("xk", [P, 8]), ("blk", [P, 8]), ("over8", [P, 8, MORE]), ("wi", [P, 8]),
                            ("tt", [P, 8]), ("isx", [P, 8]), ("item", [P, 8]),
                            ("nif", [P, 3]), ("twos", [P, XTRA // 2]), ("odd", [P, XTRA // 2]),
                            ("slot1h", [P, 8, P]), ("item1h", [P, 8, ITEMS]), ("entries", [P, 8, 3, ITEMS])):
            rt[name] = sb("r_" + name, shape, F32, o2)
            if name == "slot1h":
                at_slot1h = o2
            o2 += -(-4 * int(np.prod(shape[1:])) // 32) * 32
        assert o2 <= R0 + 60 * K
        rt["cmp"] = sb("r_cmp", [P, XTRA, 32], F32, at_slot1h)

        PS = ctx.enter_context(nc.psum_tensor("PS", [P, 8, S], F32))

        s_const, s_row, s_oh = sem("s_const"), sem("s_row"), sem("s_oh")
        s_x = [sem(f"s_x{t}") for t in range(NT)]
        s_raw = [sem(f"s_raw{i}") for i in range(RAW)]
        s_bias, s_bias_ready, s_tv, s_tvd = sem("s_bias"), sem("s_bias_ready"), sem("s_tv"), sem("s_tvd")
        s_whi, s_wlo, s_chunk = sem("s_whi"), sem("s_wlo"), sem("s_chunk")
        s_act, s_dve, s_pool, s_wrs = sem("s_act"), sem("s_dve"), sem("s_pool"), sem("s_wrs")
        s_sp_passed, s_pool_passed, s_pe_passed = sem("s_sp_passed"), sem("s_pool_passed"), sem("s_pe_passed")
        s_eps, s_maskb, s_wide, s_wide_in = sem("s_eps"), sem("s_maskb"), sem("s_wide"), sem("s_wide_in")
        s_xsq, s_xn, s_xtr, s_xhi, s_xlo = (sem(n) for n in ("s_xsq", "s_xn", "s_xtr", "s_xhi", "s_xlo"))
        (s_qhi, s_sqq, s_sqk, s_kg, s_rks, s_rqs, s_khi, s_vt, s_vtc, s_exp, s_ptc, s_ohi) = (
            sem(n) for n in ("s_qhi", "s_sqq", "s_sqk", "s_kg", "s_rks", "s_rqs", "s_khi", "s_vt", "s_vtc",
                             "s_exp", "s_ptc", "s_ohi"))
        (s_kn, s_klo, s_qlo, s_rq, s_negm, s_p, s_olo) = (
            sem(n) for n in ("s_kn", "s_klo", "s_qlo", "s_rq", "s_negm", "s_p", "s_olo"))
        (s_ksum, s_qsum, s_vtr, s_sc, s_ptr, s_pv) = (
            sem(n) for n in ("s_ksum", "s_qsum", "s_vtr", "s_sc", "s_ptr", "s_pv"))
        (s_sga, s_ta, s_sgb, s_mg, s_mhi, s_mlo) = (sem(n) for n in ("s_sga", "s_ta", "s_sgb", "s_mg", "s_mhi", "s_mlo"))
        (s_xres, s_h, s_hd, s_sqh, s_htr, s_htc, s_lg, s_wr, s_wrg) = (
            sem(n) for n in ("s_xres", "s_h", "s_hd", "s_sqh", "s_htr", "s_htc", "s_lg", "s_wr", "s_wrg"))
        (s_lgc, s_rh, s_M, s_pos, s_r1, s_r2, s_ent, s_tab, s_idx, s_tok, s_cst2) = (
            sem(n) for n in ("s_lgc", "s_rh", "s_M", "s_pos", "s_r1", "s_r2", "s_ent", "s_tab", "s_idx", "s_tok", "s_cst2"))
        s_wg = [[sem(f"s_wg{b}_{c}") for c in range(4)] for b in range(2)]
        s_wu = [sem(f"s_wu{c}") for c in range(4)]
        s_wd = [sem(f"s_wd{c}") for c in range(4)]
        (s_gu, s_dn, s_gath, s_xs, s_xt2, s_xTc, s_sgm, s_hs, s_hst, s_hTc, s_yhi, s_ylo, s_comb, s_added, s_nreg) = (
            sem(n) for n in ("s_gu", "s_dn", "s_gath", "s_xs", "s_xt2", "s_xTc", "s_sgm", "s_hs", "s_hst", "s_hTc", "s_yhi",
                             "s_ylo", "s_comb", "s_added", "s_nreg"))
        (s_out, s_xg0) = (sem(n) for n in ("s_out", "s_xg0"))

        def settle(eng, passed):
            eng.sem_inc(passed, 1)

        win = w_in.rearrange("l (k p) c -> (l p) k c", p=P)
        upa = w_up_a.rearrange("l (k p) c -> (l p) k c", p=P)
        upb = w_up_b.rearrange("l (k p) c -> (l p) k c", p=P)
        wo = w_out.rearrange("l (k p) c -> (l p) k c", p=P)
        x_v = x.rearrange("b (t p) d -> p (b t) d", p=P)
        out_v = out.rearrange("b (t p) d -> p (b t) d", p=P)
        h_v = h_d.rearrange("(t p) d -> p t d", p=P)

        block = ctx.enter_context(nc.Block())

        @block.sync
        def _(sp):
            for t in range(NT):
                sp.dma_start(xt[:, t, :], x_v[:, t, :]).then_inc(s_x[t], 16)
                if t == 0:
                    sp.dma_start(gb[:], bass.AP(norm1_g.tensor, 0, [[0, P], [1, D]])).then_inc(s_row, 16)
                    sp.dma_start(mats[:], c_mats).then_inc(s_const, 16)

            def chunk(n, src):
                if not isinstance(n, int) or n >= RAW:
                    sp.wait_ge(s_wlo, n - (RAW - 1))
                    if not isinstance(n, int):
                        settle(sp, s_sp_passed)
                slot = chunk.slot % RAW
                chunk.slot += 1
                k = src.shape[1]
                sp.dma_start(w_raw[:, slot, :].rearrange("p (k c) -> p k c", k=k), src).then_inc(s_raw[slot], 16)

            chunk.slot = 0
            for n in range(RAW):
                chunk(n, win[:, 8 * (n % 2):8 * (n % 2) + 8, ds((COL_KA, COL_VA)[n // 2], P)])
            def bias_a_by_distance():
                sp.wait_ge(s_tv, 1)
                sp.dma_start(tvec_d, tvec[:]).then_inc(s_tvd, 16)
                sp.wait_ge(s_tvd, 16)
                sp.dma_start(bias_d, bass.AP(tvec_d.tensor, P - 1, [[S, A_HEADS], [-1, P], [1, 3 * P]])).then_inc(s_tvd, 16)
                sp.dma_start(mask_b[:], c_maskb).then_inc(s_maskb, 16)

            def bias_a(hh):
                if hh:
                    sp.wait_ge(s_negm, hh)
                else:
                    sp.wait_ge(s_tvd, 32)
                sp.dma_start(bias[:, 0:2, :].rearrange("p a b -> p (a b)")[:, 0:3 * P], bias_d[hh]).then_inc(s_bias, 16)

            def bias_b(h_):
                if not isinstance(h_, int):
                    sp.wait_ge(s_bias_ready, h_)
                    settle(sp, s_sp_passed)
                sp.dma_start(wide[:].rearrange("p k c -> p (k c)"),
                             wide_d[ds(h_, 1), :, :].rearrange("o p c -> (o p) c")).then_inc(s_wide_in, 16)

            def spread(h_, r):
                sp.dma_start(wide_d[h_].rearrange("(i r) (k c) -> r k i c", r=ROWS, k=ROWS)[r],
                             bass.AP(rpb_pad.tensor, (h_ * (2 * NB_ROWS - 1) + NB_ROWS - 1 - r) * RPB_W + NB_COLS - 1,
                                     [[RPB_W, ROWS], [-1, QC], [1, 3 * QC]])).then_inc(s_wide, 16)

            n = 0
            for g in range(A_KV):
                cols = [COL_KA + HD * g, COL_VA + HD * g] + [COL_QA + HD * (A_GROUP * g + a) for a in range(A_GROUP)]
                for i, c in enumerate(cols):
                    for f in range(2):
                        if n >= RAW:
                            chunk(n, win[:, 8 * f:8 * f + 8, ds(c, P)])
                        if n == 5:
                            bias_a_by_distance()
                        if n >= 9 and (n - 9) % 12 in (0, 2, 4, 6):
                            bias_a(A_GROUP * ((n - 9) // 12) + (n - 9) % 12 // 2)
                        for i_ in range(3 * n, min(3 * n + 3, B_HEADS * ROWS)):
                            spread(i_ // ROWS, i_ % ROWS)
                        n += 1
            assert n == CH_B
            sp.wait_ge(s_wide, 16 * B_HEADS * ROWS)

            def b_head(h_, first):
                for i, c in enumerate((COL_QB, COL_KB, COL_VB)):
                    for f in range(2):
                        chunk(h_ * 6 + (CH_B + 2 * i + f), win[:, 8 * f:8 * f + 8, ds(h_ * HD + c, P)])
                        if first and f == 1 and i < 2:
                            bias_a(A_HEADS - 2 + i)
                        if i == 1 and f == 1:
                            bias_b(h_)

            b_head(0, True)
            with sp.Fori(1, B_HEADS) as h_:
                b_head(h_, False)
            with sp.Fori(0, KT) as j:
                n = j * 6 + CH_M
                c = j * P
                chunk(n, win[:, 0:8, ds(c + COL_GA, P)])
                chunk(n + 1, win[:, 8:16, ds(c + COL_GA, P)])
                chunk(n + 2, upa[:, :, ds(c, P)])
                chunk(n + 3, win[:, 0:8, ds(c + COL_GB, P)])
                chunk(n + 4, win[:, 8:16, ds(c + COL_GB, P)])
                chunk(n + 5, upb[:, :, ds(c, P)])

            wg_v = w_gate.rearrange("l e (p k) f -> p (l e) k f", p=P)
            wu_v = w_up.rearrange("l e (p k) f -> p (l e) k f", p=P)
            wd_v = w_down.rearrange("l e (j p c) n -> p (l e) j c n", j=2, p=P)

            def load_gate(e, c, odd):
                sp.dma_start((wg_s, wg_odd)[odd][:, 4 * c:4 * c + 4, :],
                             wg_v[:, ds(e, 1), 4 * c:4 * c + 4, :].rearrange("p o k f -> p (o k) f")).then_inc(s_wg[odd][c], 16)

            def load_up(e, c):
                sp.dma_start(wu_s[:, 4 * c:4 * c + 4, :], wu_v[:, ds(e, 1), 4 * c:4 * c + 4, :].rearrange("p o k f -> p (o k) f")).then_inc(s_wu[c], 16)

            def load_down(e, c):
                sp.dma_start(wd_s[:, c, :], wd_v[:, ds(e, 1), c // 2, c % 2, :].rearrange("p o n -> p (o n)")).then_inc(s_wd[c], 16)

            for nn in range(NT):
                for c in range(8):
                    chunk(CH_O + 8 * nn + c, wo[:, 2 * c:2 * c + 2, nn * S:nn * S + S])
                    if nn == 0 and c == 2:
                        sp.wait_ge(s_bias_ready, B_HEADS)
                        wr3 = wr[:]
                        sp.dma_start(wr3[:, :, 0:GROUPS],
                                     w_router_group.rearrange("l (k p) c -> (l p) k c", p=P)).then_inc(s_wr, 16)
                        sp.dma_start(wr3[:, :, GROUPS:LOG],
                                     w_router_expert.rearrange("l (k p) c -> (l p) k c", p=P)).then_inc(s_wr, 16)
                        sp.wait_ge(s_chunk, CH_O)
                    if nn == 0 and 4 <= c:
                        load_gate(0, c - 4, 0)
                    if c == 3:
                        if nn:
                            sp.wait_ge(s_h, 4 * nn)
                        else:
                            sp.wait_ge(s_mg, KT)
                        sp.dma_start(x_res[:], x_v[:, 0:3, nn * S:nn * S + S]).then_inc(s_xres, 16)
                        sp.dma_start(x_last[:], x_v[:, 3, nn * S:nn * S + S]).then_inc(s_xres, 16)
                        if nn:
                            sp.dma_start(h_v[:, :, (nn - 1) * S:nn * S], h[:, :, (nn - 1) * S:nn * S]).then_inc(s_hd, 16)
                    if nn == 1 and 4 <= c:
                        if c == 4:
                            sp.wait_ge(s_mlo, KT)
                        load_up(0, c - 4)
            sp.wait_ge(s_h, 4 * NT)
            sp.dma_start(h_v[:, :, D - S:D], h[:, :, D - S:D]).then_inc(s_hd, 16)
            for c in range(4):
                load_down(0, c)
            sp.wait_ge(s_lg, 4 * NT)
            for c in range(4):
                load_gate(1, c, 1)

            def item_loads(i, e, gate=None):
                for c in range(4):
                    sp.wait_ge(s_gu, i * 4 + (c - 3))
                    settle(sp, s_sp_passed)
                    load_up(e, c)
                    if gate is not None:
                        load_gate(gate[0], c, gate[1])
                for c in range(4):
                    sp.wait_ge(s_dn, i * 4 + (c - 3))
                    settle(sp, s_sp_passed)
                    load_down(e, c)

            item_loads(1, 1, (2, 0))
            with sp.Fori(1, EXPERTS // 2 - 1) as p:
                item_loads(p * 2, p * 2, (p * 2 + 1, 1))
                item_loads(p * 2 + 1, p * 2 + 1, (p * 2 + 2, 0))
            item_loads(EXPERTS - 2, EXPERTS - 2, (EXPERTS - 1, 1))
            item_loads(EXPERTS - 1, EXPERTS - 1)
            sp.wait_ge(s_r2, 1)
            extra_pairs = sp.value_load(nitem[0:1, 1:2], min_val=0, max_val=XTRA // 2)
            with sp.If(extra_pairs > 0):
                with sp.Fori(0, extra_pairs) as p:
                    for odd in range(2):
                        e = sp.value_load(eid[0:1, ds(p * 2 + odd, 1)], min_val=0, max_val=EXPERTS - 1)
                        item_loads(p * 2 + (EXPERTS + odd), e, (e, odd))
            items = sp.value_load(nitem[0:1, 0:1], min_val=EXPERTS, max_val=EXPERTS + XTRA)
            for t in range(NT):
                sp.wait_ge(s_added, items * 4 + (2 * t + 4))
                settle(sp, s_sp_passed)
                sp.dma_start(out_v[:, t, :], h[:, t, :]).then_inc(s_out, 16)
            sp.wait_ge(s_out, 16 * NT)

        @block.gpsimd
        def _(pool):
            pool.memset(eps[:, 0:1], EPS).then_inc(s_eps, 1)
            pool.memset(eps[:, 1:2], EPS * HD).then_inc(s_eps, 1)
            gp = pool
            gp.dma_start(onehot[:], c_onehot).then_inc(s_oh, 16)
            gp.dma_start(mask_a[:], c_maska).then_inc(s_oh, 16)
            gp.dma_start(small["table"][0:BUCKETS, :], rel_bias_table).then_inc(s_oh, 16)
            for i, (qn, kk) in enumerate(((q_norm_a, k_norm_a), (q_norm_b, k_norm_b))):
                gp.dma_start(gq[:, i:i + 1], qn.rearrange("l d -> d l"), allow_slow_non_contiguous=True).then_inc(s_cst2, 16)
                gp.dma_start(gk[:, i:i + 1], kk.rearrange("l d -> d l"), allow_slow_non_contiguous=True).then_inc(s_cst2, 16)
            gp.dma_start(sink[:], bass.AP(sink_a.tensor, 0, [[0, P], [1, A_HEADS]])).then_inc(s_cst2, 16)
            gp.dma_start(g2m[:], norm2_g.rearrange("l (p k) -> (l p) k", p=P)).then_inc(s_wrg, 16)
            gp.dma_start(g2c[:], norm2_g.rearrange("l (k p) -> (l p) k", p=P), allow_slow_non_contiguous=True).then_inc(s_wrg, 16)
            gp.dma_start(rb[:, 0:GROUPS], bass.AP(b_router_group.tensor, 0, [[0, P], [1, GROUPS]])).then_inc(s_wrg, 16)
            gp.dma_start(rb[:, GROUPS:LOG], bass.AP(b_router_expert.tensor, 0, [[0, P], [1, EXPERTS]])).then_inc(s_wrg, 16)
            gp.dma_start(ramp4[:], c_ramp[:, 0:16]).then_inc(s_wrg, 16)
            pool.wait_ge(s_maskb, 16)
            with pool.Fori(0, B_HEADS) as h_:
                pool.wait_ge(s_wide_in, h_ * 16 + 16)
                pool.wait_ge(s_negm, h_ + A_HEADS)
                for kind in range(3):
                    ins = nc.gpsimd.tensor_tensor(bias[:, kind, :].rearrange("p (c k) -> p k c", k=ROWS),
                                                  wide[:, :, QC - 8 * kind:QC - 8 * kind + KC],
                                                  mask_b[:, kind, :].rearrange("p (k c) -> p k c", k=ROWS), ALU.add)
                ins.then_inc(s_bias_ready, 1)
            pool.wait_ge(s_bias_ready, B_HEADS)
            gp.dma_start(rt["ramp"][:].rearrange("p a b -> p (a b)"), c_ramp[:, 32:32 + 128]).then_inc(s_idx, 16)
            gp.dma_start(rt["iota"][:], c_ramp[:, 160:160 + SLOTS]).then_inc(s_idx, 16)
            gp.dma_start(rt["ent"][:].rearrange("p a b -> p (a b)"), c_entry).then_inc(s_idx, 16)
            pool.wait_ge(s_chunk, CH_END)
            gp.dma_start(token[:], c_tokens).then_inc(s_tok, 16)
            nc.gpsimd.memset(xg[:], 0.0).then_inc(s_xg0, 1)
            pool.wait_ge(s_r1, 1)
            items = pool.value_load(nitem[0:1, 0:1], min_val=EXPERTS, max_val=EXPERTS + XTRA)
            pool.wait_ge(s_hd, 16 * NT)
            pool.wait_ge(s_xg0, 1)
            pool.wait_ge(s_nreg, 1)

            nc.gpsimd.tensor_copy(cur_x[:], idx_x[:, 0:1]).then_inc(s_pool, 1)
            pool.wait_ge(s_pool, 1)
            gp.indirect_dma_start(xg[:], None, h_d, bass.IndirectOffsetOnAxis(ap=cur_x[:, 0:1], axis=0),
                                  bounds_check=S - 1, oob_is_err=False).then_inc(s_gath, 16)
            with pool.Fori(0, items) as i:
                pool.wait_ge(s_gath, i * 16 + 16)
                nc.gpsimd.tensor_copy(cur_x[:], idx_x[:, ds(i + 1, 1)]).then_inc(s_pool, 1)
                pool.wait_ge(s_pool, i + 2)
                pool.wait_ge(s_xt2, i + 1)
                settle(pool, s_pool_passed)
                gp.indirect_dma_start(xg[:], None, h_d, bass.IndirectOffsetOnAxis(ap=cur_x[:, 0:1], axis=0),
                                      bounds_check=S - 1, oob_is_err=False).then_inc(s_gath, 16)

        def grid(ap, kind):
            return ap if kind == 0 else ap.rearrange("p (r c) -> p r c", r=ROWS)

        def tokens(buf, kind):
            return buf[:] if kind == 0 else buf[:].rearrange("p (c r) -> p r c", r=ROWS)

        def o_view(buf, hh, kind):
            v = buf[:, ds(hh, 1), :]
            if kind == 0:
                return v.rearrange("p o c -> p (o c)")
            return v.rearrange("p o (r c) -> p (o c) r", r=ROWS)

        def o_psum(kind):
            return PS[:, 6, :] if kind == 0 else PS[:, 6, :].rearrange("p (c r) -> p c r", r=ROWS)

        @block.scalar
        def _(act):
            own = Chain(act, s_act)
            act_fn = nc.scalar.activation
            act.wait_ge(s_eps, 2)
            act_fn(es[:, 0:1], eps[:, 0:1], ACT.Sqrt, bias=eps[:, 0:1])

            def x_rms(t):
                act.wait_ge(s_x[t], 16)
                own.do(act_fn(junk[:], xt[:, t, :], ACT.Square, accum_out=ssx[:, t:t + 1]))
                act_fn(rsx[:, t:t + 1], ssx[:, t:t + 1], ACT.Sqrt, bias=eps[:, 0:1], scale=1.0 / D).then_inc(s_xsq, 1)

            def x_upper(t):
                for G in range(4 * t, 4 * t + 4):
                    kk = G % 4
                    act.wait_ge(s_xtr, G + 1)
                    act_fn(x_hi[:, 4 * kk:4 * kk + 4, t * P:t * P + P],
                           PS[:, G % 8, :].rearrange("p (k c) -> p k c", k=4), ACT.Copy).then_inc(s_xhi, 1)

            def split(n, python_n):
                r, b = python_n % RAW, python_n % SPLIT
                act.wait_ge(s_raw[r], (n - r) // RAW * 16 + 16 if isinstance(n, int) else split.raw(n, r))
                if not isinstance(n, int) or n >= SPLIT:
                    act.wait_ge(s_chunk, n - (SPLIT - 1))
                act_fn(w_hi[:, b, :], w_raw[:, r, :], ACT.Copy).then_inc(s_whi, 1)

            def q_tile(hh, bank, kind, need, vtr, first=False):
                act.wait_ge(s_chunk, need)
                if not first:
                    act.wait_ge(s_sc, hh)
                act_fn(tokens(q_hi, kind), grid(PS[:, bank, :], kind), ACT.Copy,
                       scale=gq[:, kind:kind + 1]).then_inc(s_qhi, 1)
                act.wait_ge(s_vtr, vtr)
                if not first:
                    act.wait_ge(s_qsum, hh)
                act_fn(tokens(sq, kind), grid(PS[:, bank, :], kind), ACT.Square).then_inc(s_sqq, 1)

            def q_root(hh, kind, first=False):
                act.wait_ge(s_qsum, hh + 1)
                if not first:
                    act.wait_ge(s_rq, hh)
                col = PS[:, 7 if kind == 0 else 4, 0:4]
                act_fn(rqs[:], col, ACT.Sqrt, bias=eps[:, 1:2]).then_inc(s_rqs, 1)

            def k_tile(kv, hh, bank, kind, need, first=False):
                act.wait_ge(s_chunk, need)
                if not first:
                    act.wait_ge(s_klo, kv)
                    act.wait_ge(s_qsum, hh)
                act_fn(kn[:], PS[:, bank, :], ACT.Copy, scale=gk[:, kind:kind + 1]).then_inc(s_kg, 1)
                act_fn(sq[:], PS[:, bank, :], ACT.Square).then_inc(s_sqk, 1)

            def k_root(kv, bank, p_used):
                act.wait_ge(s_ksum, kv + 1)
                if p_used is not None:
                    act.wait_ge(s_ptr, p_used)
                act_fn(rk[:], PS[:, bank, :], ACT.Sqrt, bias=eps[:, 0:1], scale=1.0 / HD).then_inc(s_rks, 1)

            def k_split(kv, kind, sc_used):
                act.wait_ge(s_kn, kv + 1)
                if sc_used is not None:
                    act.wait_ge(s_sc, sc_used)
                act_fn(tokens(k_hi, kind), grid(kn[:], kind), ACT.Copy).then_inc(s_khi, 1)

            def v_tile(kv, kind, bank, need):
                act.wait_ge(s_chunk, need)
                act.wait_ge(s_ksum, kv + 1)
                act_fn(tokens(vt, kind), grid(PS[:, bank, :], kind), ACT.Copy).then_inc(s_vt, 1)

            def v_copy(kv, src, pv_used):
                act.wait_ge(s_vtr, kv + 1)
                if pv_used is not None:
                    act.wait_ge(s_pv, pv_used)
                n = src.shape[1]
                act_fn(v_t[:, 0:n // P, :].rearrange("p a b -> p (a b)"), src, ACT.Copy).then_inc(s_vtc, 1)

            def exps(hh, kind, bias_col):
                act.wait_ge(s_negm, hh + 1)
                for b in range(NT):
                    lo, hi = a_keys(b) if kind == 0 else (0, 2 * P)
                    ins = act_fn(prob[:, b, lo:hi], prob[:, b, lo:hi], ACT.Exp, bias=negm[:, b:b + 1],
                                 accum_out=den[:, b:b + 1])
                    if kind or b < NT - 1:
                        ins.then_inc(s_exp, 1)
                if kind == 0:
                    act_fn(es[:], negm[:], ACT.Exp, bias=bias_col).then_inc(s_exp, 1)

            def p_copy(hh, kind, first=False):
                act.wait_ge(s_ptr, hh + 1)
                if not first:
                    act.wait_ge(s_pv, hh)
                if kind == 0:
                    act_fn(p_t[:, 0, P:3 * P], PS[:, 2, P:3 * P], ACT.Copy)
                    act_fn(p_t[:, 3, 0:2 * P], PS[:, 5, 0:2 * P], ACT.Copy)
                    act_fn(p_t[:, 1:3, :], PS[:, 3:5, 0:3 * P], ACT.Copy).then_inc(s_ptc, 1)
                else:
                    act_fn(p_t[:, :, 0:2 * P], PS[:, 4:6, :].rearrange("p a (b c) -> p (a b) c", b=2),
                           ACT.Copy).then_inc(s_ptc, 1)

            def o_split(hh, kind):
                act.wait_ge(s_pv, hh + 1)
                act_fn(o_view(o_hi, hh, kind), o_psum(kind), ACT.Copy).then_inc(s_ohi, 1)

            x_rms(0)
            x_rms(1)
            x_rms(2)
            x_upper(0)
            x_rms(3)
            x_upper(1)
            x_upper(2)
            split(0, 0)
            x_upper(3)
            act.wait_ge(s_cst2, 5 * 16)
            for g in range(A_KV):
                for s in range(12):
                    n = 12 * g + s
                    split(n + 1, n + 1)
                    tail_head = A_GROUP * g - 1
                    if s == 0 and g:
                        q_tile(tail_head, 1, 0, n, g)
                        p_copy(tail_head - 1, 0)
                    if s == 1 and g:
                        o_split(tail_head - 1, 0)
                        q_root(tail_head, 0)
                        exps(tail_head, 0, sink[:, tail_head:tail_head + 1])
                    if s == 2:
                        k_tile(g, A_GROUP * g, 0, 0, n, first=(g == 0))
                        if g:
                            p_copy(tail_head, 0)
                    if s == 3:
                        if g:
                            o_split(tail_head, 0)
                        k_root(g, 7, A_GROUP * g if g else None)
                    if s == 4:
                        k_split(g, 0, A_GROUP * g if g else None)
                        v_tile(g, 0, 1, n)
                    if s == 5:
                        v_copy(g, PS[:, 7, :], A_GROUP * g if g else None)
                    if s >= 6 and s % 2 == 0:
                        a = (s - 6) // 2
                        hh = A_GROUP * g + a
                        q_tile(hh, a % 2, 0, n, g + 1, first=(hh == 0))
                        if a:
                            p_copy(hh - 1, 0, first=(hh == 1))
                    if s >= 7 and s % 2 == 1:
                        a = (s - 7) // 2
                        hh = A_GROUP * g + a
                        if a:
                            o_split(hh - 1, 0)
                        q_root(hh, 0, first=(hh == 0))
                        exps(hh, 0, sink[:, hh:hh + 1])
            split.raw = lambda n, r: None

            def b_steps(h_, first):
                hh = h_ + A_HEADS
                kv = h_ + A_KV
                c0 = h_ * 6 + CH_B
                for s in range(6):
                    nxt = s + 1
                    split.raw = lambda n, r, nxt=nxt: h_ * 32 + (16 * ((CH_B + nxt - r) // RAW) + 16)
                    split(c0 + nxt, CH_B + nxt)
                    if s == 0:
                        if first:
                            q_tile(A_HEADS - 1, 1, 0, c0, A_KV)
                            p_copy(A_HEADS - 2, 0)
                        else:
                            k_split(kv - 1, 1, hh - 1)
                            v_tile(kv - 1, 1, 7, c0)
                    if s == 1:
                        if first:
                            o_split(A_HEADS - 2, 0)
                            q_root(A_HEADS - 1, 0)
                            exps(A_HEADS - 1, 0, sink[:, A_HEADS - 1:A_HEADS])
                        else:
                            v_copy(kv - 1, PS[:, 4:6, :].rearrange("p a b -> p (a b)"), hh - 1)
                            exps(hh - 1, 1, None)
                    if s == 2:
                        q_tile(hh, 0, 1, c0 + 2, kv)
                        p_copy(hh - 1, 0 if first else 1)
                    if s == 3:
                        o_split(hh - 1, 0 if first else 1)
                        q_root(hh, 1)
                    if s == 4:
                        k_tile(kv, hh + 1, 1, 1, c0 + 4)
                    if s == 5:
                        k_root(kv, 6, hh)

            b_steps(0, True)
            with act.Fori(1, B_HEADS) as h_:
                b_steps(h_, False)

            def m_steps(j, first):
                c0 = j * 6 + CH_M
                hh, kv = HEADS, A_KV + B_HEADS
                for s in range(6):
                    nxt = s + 1
                    split.raw = lambda n, r, nxt=nxt: j * 32 + (16 * ((CH_M + nxt - r) // RAW) + 16)
                    split(c0 + nxt, CH_M + nxt)
                    if first and s == 0:
                        k_split(kv - 1, 1, hh - 1)
                        v_tile(kv - 1, 1, 7, c0)
                    if first and s == 1:
                        v_copy(kv - 1, PS[:, 4:6, :].rearrange("p a b -> p (a b)"), hh - 1)
                        exps(hh - 1, 1, None)
                    if first and s == 2:
                        p_copy(hh - 1, 1)
                        act.wait_ge(s_vtr, kv)
                        act.wait_ge(s_qsum, hh)
                    if s == 2:
                        if not first:
                            act.wait_ge(s_ta, j)
                        act.wait_ge(s_chunk, c0 + 2)
                        act_fn(sig_a[:], PS[:, 0, :], ACT.Sigmoid).then_inc(s_sga, 1)
                    if first and s == 3:
                        o_split(hh - 1, 1)
                    if s == 5:
                        if not first:
                            act.wait_ge(s_mg, j)
                        act.wait_ge(s_chunk, c0 + 5)
                        act_fn(sig_b[:], PS[:, 7, :], ACT.Sigmoid).then_inc(s_sgb, 1)

            m_steps(0, True)
            with act.Fori(1, KT) as j:
                m_steps(j, False)

            def merged_split(j):
                act.wait_ge(s_mg, j + 1)
                act_fn(m_hi[:, j, :], m_raw[:, j, :], ACT.Copy).then_inc(s_mhi, 1)

            act.wait_ge(s_chunk, CH_O - 1)
            merged_split(0)
            merged_split(1)

            def h_squares(nn):
                for t in range(NT):
                    act.wait_ge(s_h, 4 * nn + t + 1)
                    if nn or t:
                        act.wait_ge(s_sqh, 4 * nn + t)
                    act_fn(PS[:, 6, :], h[:, t, nn * S:nn * S + S], ACT.Square,
                           accum_out=ssh[:, 4 * t + nn:4 * t + nn + 1]).then_inc(s_sqh, 1)

            def h_copy(k):
                act.wait_ge(s_htr, k + 1)
                if k >= 2:
                    act.wait_ge(s_lg, k - 1)
                act_fn((h_t, h_t2)[k % 2][:], PS[:, 4 + k % 2, :], ACT.Copy).then_inc(s_htc, 1)

            for nn in range(NT):
                for c in range(8):
                    n = CH_O + 8 * nn + c
                    if n + 1 < CH_END:
                        split(n + 1, n + 1)
                    if nn == 0 and c < 7:
                        merged_split(2 * c + 2)
                        merged_split(2 * c + 3)
                    if nn and c == 0:
                        h_squares(nn - 1)
                    if nn and 2 <= c < 6:
                        h_copy(4 * (nn - 1) + c - 2)
            h_squares(NT - 1)
            for k in range(4 * NT - 4, 4 * NT):
                if k == 4 * NT - 1:
                    act.wait_ge(s_M, 1)
                    act_fn(rhs_[:], ssum[:], ACT.Sqrt, bias=eps[:, 0:1], scale=1.0 / D).then_inc(s_rh, 1)
                h_copy(k)
            act.wait_ge(s_M, 2)
            act_fn(rt["eg"][:], rt["gd"][:], ACT.Exp).then_inc(s_lgc, 1)
            act.wait_ge(s_M, 4)
            act_fn(rt["e2"][:], rt["e2"][:], ACT.Exp).then_inc(s_lgc, 1)
            act.wait_ge(s_r1, 1)
            pairs = act.value_load(nitem[0:1, 2:3], min_val=EXPERTS // 2, max_val=(EXPERTS + XTRA) // 2)
            act.wait_ge(s_nreg, 1)

            def rows_scaled(i):
                act.wait_ge(s_gath, i * 16 + 16)
                act_fn(xg[:], xg[:], ACT.Copy, scale=tab[0:SLOTS, 2, ds(i, 1)]).then_inc(s_xs, 1)

            rows_scaled(0)
            with act.Fori(0, pairs) as p:
                for odd in range(2):
                    i = p * 2 + odd
                    rows_scaled(i + 1)
                    act.wait_ge(s_gu, i * 4 + 4)
                    act_fn(sg[:], PS[:, 0, 0:F // 2], ACT.Sigmoid).then_inc(s_sgm, 1)
                    act.wait_ge(s_dn, i * 4 + 4)
                    act.wait_ge(s_comb, p * 8 + 8)
                    for f in range(2):
                        q = slice(SLOTS * (f ^ odd), SLOTS * (f ^ odd) + SLOTS)
                        last = act_fn(y_hi[f][q, :], PS[q, 4:6, :].rearrange("p a b -> p (a b)"), ACT.Copy,
                                      scale=tab[q, 1, ds(i, 1)])
                    last.then_inc(s_yhi, 1)

        def routing(dve, own, V):
            R = rt
            a = {k: v[:] for k, v in rt.items()}
            tt, ts, stt = V.tensor_tensor, V.tensor_scalar, V.scalar_tensor_tensor

            def top(sc, best, ramp, sel, n, tmp_score, tmp_max):
                own.do(V.reduce_max(best, sc, AX))
                own.do(tt(tmp_score, sc, bc(best, n), ALU.subtract))
                own.do(stt(out=tmp_score, in0=tmp_score, scalar=0.0, in1=ramp, op0=ALU.is_equal, op1=ALU.mult))
                own.do(V.reduce_max(tmp_max, tmp_score, AX))
                own.do(tt(sel, tmp_score, bc(tmp_max, n), ALU.is_equal))

            for name in ("nb", "xa", "xb"):
                own.link(V.memset(R[name][:, 0:16], 0.0))
            own.link(V.memset(R["before"][:, 0, :], 0.0))
            dve.wait_ge(s_sqh, 16)
            V.reduce_sum(ssum[:], ssh[:].rearrange("p (t n) -> p t n", t=NT), AX).then_inc(s_M, 1)
            dve.wait_ge(s_rh, 1)
            own.do(V.reciprocal(rh[:], rhs_[:]))
            dve.wait_ge(s_idx, 48)
            own.do(V.tensor_copy(R["ent"][:, 2, :].rearrange("p (k t) -> p k t", k=2), rep(rh[:], 2)))
            own.link(ts(a["twos"], a["iota"][:, 0:XTRA // 2], 2.0, None, ALU.mult))
            own.do(ts(a["steps"], a["iota"][:, 1:MORE + 1], float(SLOTS), None, ALU.mult))
            dve.wait_ge(s_lg, 4 * NT)
            for t in range(NT):
                own.link(stt(out=R["L"][:, t, :], in0=PS[:, 7, t * LOG:t * LOG + LOG], scalar=rh[:, t:t + 1], in1=rb[:],
                             op0=ALU.mult, op1=ALU.add))
            own.wait()
            g = R["L"][:, :, 0:GROUPS]
            e = R["L"][:, :, GROUPS:LOG].rearrange("p t (g e) -> p t g e", g=GROUPS)
            ramp4v = ramp4[:].rearrange("p (t g) -> p t g", t=NT)
            own.do(V.reduce_max(a["gm"], g, AX))
            tt(a["gd"], g, bc(a["gm"], 4), ALU.subtract).then_inc(s_M, 1)
            dve.wait_ge(s_M, 2)
            own.do(stt(out=a["gs"], in0=a["gd"], scalar=0.0, in1=ramp4v, op0=ALU.is_equal, op1=ALU.mult))
            own.do(V.reduce_max(a["gx"], a["gs"], AX))
            own.do(tt(a["oh"], a["gs"], bc(a["gx"], 4), ALU.is_equal))
            own.do(ts(a["pen"], a["oh"], -1.0, -NEG, ALU.add, ALU.mult))
            own.do(tt(a["em"].rearrange("p t (g e) -> p t g e", g=GROUPS), e, bc(a["pen"], PER_GROUP), ALU.add))
            M1, M2 = R["M12"][:, 0, :, :], R["M12"][:, 1, :, :]
            top(a["em"], a["v1"], a["ramp"], M1, 32, a["s1"], a["x1"])
            own.do(stt(out=a["em2"], in0=M1, scalar=2 * NEG, in1=a["em"], op0=ALU.mult, op1=ALU.add))
            top(a["em2"], a["v2"], a["ramp"], M2, 32, a["s1"], a["x1"])
            own.do(tt(a["Ms"], M1, M2, ALU.add))
            before = R["before"]
            own.do(V.tensor_copy(before[:, 1, :], R["Ms"][:, 0, :]))
            for t in range(1, NT):
                own.do(tt(before[:, t + 1, :], before[:, t, :], R["Ms"][:, t, :], ALU.add))
            dve.sem_inc(s_M, 1)
            tt(a["e2"], a["v2"], a["v1"], ALU.subtract).then_inc(s_M, 1)
            M = a["M12"].rearrange("p k t e -> p (k t) e")
            prf = a["pr"].rearrange("p k t e -> p (k t) e")
            own.do(tt(prf, M, rep(a["iota"][:, 0:EXPERTS], 8), ALU.mult))
            own.do(V.reduce_sum(a["ek"], prf, AX))
            dve.wait_ge(s_lgc, 2)
            own.do(V.reduce_sum(a["sgm"], a["eg"], AX))
            own.do(V.reciprocal(a["pg"], a["sgm"]))
            own.do(ts(a["dn"], a["e2"], 1.0, None, ALU.add))
            own.do(V.reciprocal(a["rr"], a["dn"]))
            own.do(tt(R["w12"][:, 0, :], a["pg"], a["rr"], ALU.mult))
            own.do(tt(R["w12"][:, 1, :], R["w12"][:, 0, :], a["e2"], ALU.mult))
            own.do(V.tensor_copy(R["ent"][:, 1, :], a["w12"].rearrange("p k t -> p (k t)")))
            dve.wait_ge(s_pos, 2)
            counts, ranks = PS[:, 1, 128:160], PS[:, 1, 0:128]
            own.do(tt(a["over"], bc(counts, MORE), rep(a["steps"], EXPERTS), ALU.is_gt))
            nb = R["nb"][:, 16:48]
            own.do(V.reduce_sum(nb, a["over"], AX))
            src, free = "nb", ["xa", "xb"]
            for sh in (1, 2, 4, 8, 16):
                dst = free[0]
                own.do(tt(R[dst][:, 16:48], R[src][:, 16:48], R[src][:, 16 - sh:48 - sh], ALU.add))
                src, free = dst, free[::-1]
            upto = R[src]
            own.do(tt(a["xo"], upto[:, 16:48], nb, ALU.subtract))
            for k in range(2):
                own.link(tt(R["pr"][:, k, :, :].rearrange("p t e -> p (t e)"), R["M12"][:, k, :, :].rearrange("p t e -> p (t e)"),
                            ranks, ALU.mult))
            own.wait()
            own.do(V.reduce_sum(a["pk"], prf, AX))
            own.do(tt(prf, M, rep(a["xo"], 8), ALU.mult))
            own.do(V.reduce_sum(a["xk"], prf, AX))
            own.do(tt(a["over8"], bc(a["pk"], MORE), rep(a["steps"], 8), ALU.is_ge))
            b = a["blk"]
            own.do(V.reduce_sum(b, a["over8"], AX))
            own.do(stt(out=a["wi"], in0=b, scalar=-float(SLOTS), in1=a["pk"], op0=ALU.mult, op1=ALU.add))
            own.do(ts(a["isx"], b, 0.0, None, ALU.is_gt))
            own.do(tt(a["tt"], a["xk"], b, ALU.add))
            own.do(stt(out=a["tt"], in0=a["tt"], scalar=float(EXPERTS - 1), in1=a["ek"], op0=ALU.add, op1=ALU.subtract))
            own.do(tt(a["tt"], a["tt"], a["isx"], ALU.mult))
            own.do(tt(a["item"], a["tt"], a["ek"], ALU.add))
            wi3 = bass.AP(a["wi"].tensor, a["wi"].offset, [list(x) for x in a["wi"].ap] + [[0, 2], [0, SLOTS]])
            io3 = bass.AP(a["iota"].tensor, a["iota"].offset, [list(a["iota"].ap[0]), [0, 8], [0, 2], [1, SLOTS]])
            own.link(tt(a["slot1h"].rearrange("p j (f s) -> p j f s", f=2), io3, wi3, ALU.is_equal))
            own.do(tt(a["item1h"], rep(a["iota"][:, 0:ITEMS], 8), bc(a["item"], ITEMS), ALU.is_equal))
            for c in range(3):
                ins = tt(R["entries"][:, :, c, :], a["item1h"], bc(R["ent"][:, c, :], ITEMS), ALU.mult)
            ins.then_inc(s_ent, 1)
            own.do(tt(a["odd"], a["twos"], wide_of(upto[:, 47:48], XTRA // 2), ALU.is_lt))
            xp = R["nif"][:, 1:2]
            own.do(V.reduce_sum(xp, a["odd"], AX))
            own.link(ts(R["nif"][:, 0:1], xp, 2.0, float(EXPERTS), ALU.mult, ALU.add))
            own.do(ts(R["nif"][:, 2:3], xp, float(EXPERTS // 2), None, ALU.add))
            V.tensor_copy(nitem[:], a["nif"]).then_inc(s_r1, 1)
            dve.wait_ge(s_tab, 1)
            tab_ps = PS[:, 0, 0:3 * ITEMS].rearrange("p (c i) -> p c i", c=3)
            own.do(ts(idx_x[:], tab_ps[0:SLOTS, 0, :], 2.0 * S, None, ALU.add))
            own.do(ts(tab[:, 0, :], tab_ps[:, 0, :], 2.0 * S, None, ALU.add))
            own.do(V.tensor_copy(tab[:, 1:3, :], tab_ps[:, 1:3, :]))
            dve.sem_inc(s_nreg, 1)
            own.do(tt(a["cmp"], rep(upto[:, 16:48], XTRA), bc(R["iota"][:, 0:XTRA], EXPERTS), ALU.is_le))
            own.do(V.reduce_sum(a["eidf"], a["cmp"], AX))
            own.do(ts(a["eidf"], a["eidf"], float(EXPERTS - 1), None, ALU.min))
            V.tensor_copy(eid[:], a["eidf"]).then_inc(s_r2, 1)

        @block.vector
        def _(dve):
            own = Chain(dve, s_dve)
            V = nc.vector

            def x_scale(t):
                dve.wait_ge(s_xsq, t + 1)
                if t == 0:
                    dve.wait_ge(s_row, 16)
                own.do(V.reciprocal(rx[:, t:t + 1], rsx[:, t:t + 1]))
                V.scalar_tensor_tensor(out=xt[:, t, :], in0=xt[:, t, :], scalar=rx[:, t:t + 1], in1=gb[:],
                                       op0=ALU.mult, op1=ALU.mult).then_inc(s_xn, 1)

            def x_lower(t):
                for G in range(4 * t, 4 * t + 4):
                    kk = G % 4
                    dve.wait_ge(s_xhi, G + 1)
                    hi = x_hi[:, 4 * kk:4 * kk + 4, t * P:t * P + P].bitcast(F32)
                    V.tensor_tensor(x_lo[:, 4 * kk:4 * kk + 4, t * P:t * P + P],
                                    PS[:, G % 8, :].rearrange("p (k c) -> p k c", k=4), hi, ALU.subtract).then_inc(s_xlo, 1)

            def split(n, python_n):
                r, b = python_n % RAW, python_n % SPLIT
                dve.wait_ge(s_whi, n + 1)
                V.tensor_tensor(w_lo[:, b, :], w_raw[:, r, :], w_hi[:, b, :].bitcast(F32), ALU.subtract).then_inc(s_wlo, 1)

            def q_tile(hh, bank, kind):
                dve.wait_ge(s_qhi, hh + 1)
                dve.wait_ge(s_sqq, hh + 1)
                V.scalar_tensor_tensor(out=tokens(q_lo, kind), in0=grid(PS[:, bank, :], kind),
                                       scalar=gq[:, kind:kind + 1], in1=tokens(q_hi, kind).bitcast(F32), op0=ALU.mult, op1=ALU.subtract).then_inc(s_qlo, 1)

            def softmax(hh, kind, hcol):
                dve.wait_ge(s_rqs, hh + 1)
                V.reciprocal(rq[:], rqs[:]).then_inc(s_rq, 1)
                dve.wait_ge(s_rq, hh + 1)
                dve.wait_ge(s_sc, hh + 1)
                if kind == 0:
                    dve.wait_ge(s_bias, (hh + 1) * 16)
                else:
                    dve.wait_ge(s_bias_ready, hh - (A_HEADS - 1))
                for b in range(NT):
                    lo, hi = a_keys(b) if kind == 0 else (0, 2 * P)
                    if kind == 0:
                        src, bs = PS[:, 2 + b, lo:hi], bias[:, 0:2, :].rearrange("p a b -> p (a b)")[:, lo:hi]
                    else:
                        src, bs = PS[:, 2 + b // 2, (b % 2) * 256:(b % 2) * 256 + 256], bias[:, B_KIND[b], :]
                    own.link(V.scalar_tensor_tensor(out=prob[:, b, lo:hi], in0=src, scalar=rq[:, b:b + 1], in1=bs,
                                                    op0=ALU.mult, op1=ALU.add))
                for b in range(NT):
                    lo, hi = a_keys(b) if kind == 0 else (0, 2 * P)
                    own.wait(3)
                    own.link(V.reduce_max(mx[:, b:b + 1], prob[:, b, lo:hi], AX))
                own.wait()
                if kind == 0:
                    V.tensor_scalar(negm[:], mx[:], hcol, -1.0, ALU.max, ALU.mult).then_inc(s_negm, 1)
                else:
                    V.tensor_scalar(negm[:], mx[:], -1.0, None, ALU.mult).then_inc(s_negm, 1)

            def normalise(hh, kind):
                dve.wait_ge(s_exp, (hh + 1) * 4)
                if kind == 0:
                    own.do(V.tensor_tensor(den[:], den[:], es[:], ALU.add))
                own.do(V.reciprocal(rden[:], den[:]))
                for b in range(NT):
                    lo, hi = a_keys(b) if kind == 0 else (0, 2 * P)
                    ins = V.tensor_scalar(prob[:, b, lo:hi], prob[:, b, lo:hi], rden[:, b:b + 1], None, ALU.mult)
                    ins.then_inc(s_p, 1)

            def k_norm(kv):
                dve.wait_ge(s_rks, kv + 1)
                own.do(V.reciprocal(rk[:], rk[:]))
                V.tensor_tensor(kn[:], kn[:], rk[:], ALU.mult).then_inc(s_kn, 1)

            def k_split(kv, kind):
                dve.wait_ge(s_khi, kv + 1)
                V.tensor_tensor(tokens(k_lo, kind), grid(kn[:], kind), tokens(k_hi, kind).bitcast(F32),
                                ALU.subtract).then_inc(s_klo, 1)

            def o_split(hh, kind):
                dve.wait_ge(s_ohi, hh + 1)
                V.tensor_tensor(o_view(o_lo, hh, kind), o_psum(kind), o_view(o_hi, hh, kind).bitcast(F32),
                                ALU.subtract).then_inc(s_olo, 1)

            x_scale(0)
            x_scale(1)
            x_lower(0)
            x_scale(2)
            x_lower(1)
            x_scale(3)
            x_lower(2)
            split(0, 0)
            x_lower(3)

            for g in range(A_KV):
                for s in range(12):
                    split(12 * g + s + 1, 12 * g + s + 1)
                    last = A_GROUP * g - 1
                    if g == 0 and s == 0:
                        dve.wait_ge(s_pos, 1)
                        V.tensor_tensor(tvec[:], PS[0:A_HEADS, 7, :], mask_a[:], ALU.add).then_inc(s_tv, 1)
                    if s == 0 and g:
                        q_tile(last, 1, 0)
                    if s == 1 and g:
                        o_split(last - 1, 0)
                        softmax(last, 0, sink[:, last:last + 1])
                        normalise(last, 0)
                    if s == 3:
                        if g:
                            o_split(last, 0)
                        k_norm(g)
                    if s == 4:
                        k_split(g, 0)
                    if s >= 6 and s % 2 == 0:
                        a = (s - 6) // 2
                        q_tile(A_GROUP * g + a, a % 2, 0)
                    if s >= 7 and s % 2 == 1:
                        a = (s - 7) // 2
                        hh = A_GROUP * g + a
                        if a:
                            o_split(hh - 1, 0)
                        softmax(hh, 0, sink[:, hh:hh + 1])
                        normalise(hh, 0)

            def b_steps(h_, first):
                hh, kv, c0 = h_ + A_HEADS, h_ + A_KV, h_ * 6 + CH_B
                for s in range(6):
                    split(c0 + (s + 1), CH_B + s + 1)
                    if s == 0:
                        if first:
                            q_tile(A_HEADS - 1, 1, 0)
                        else:
                            k_split(kv - 1, 1)
                    if s == 1:
                        if first:
                            o_split(A_HEADS - 2, 0)
                            softmax(A_HEADS - 1, 0, sink[:, A_HEADS - 1:A_HEADS])
                            normalise(A_HEADS - 1, 0)
                        else:
                            softmax(hh - 1, 1, None)
                            normalise(hh - 1, 1)
                    if s == 2:
                        q_tile(hh, 0, 1)
                    if s == 3:
                        o_split(hh - 1, 0 if first else 1)
                    if s == 5:
                        k_norm(kv)

            b_steps(0, True)
            with dve.Fori(1, B_HEADS) as h_:
                own.loop(h_, 1, 10)
                b_steps(h_, False)
            own.done(B_HEADS - 1)

            def merge_b(j):
                dve.wait_ge(s_sgb, j + 1)
                dve.wait_ge(s_ta, j + 1)
                dve.wait_ge(s_chunk, j * 6 + (CH_M + 6))
                own.do(V.tensor_tensor(sig_b[:], sig_b[:], PS[:, 6, :], ALU.mult))
                out_ap = m_raw[:, j, :] if isinstance(j, int) else m_raw[:, ds(j, 1), :].rearrange("p o c -> p (o c)")
                V.tensor_tensor(out_ap, t_a[:], sig_b[:], ALU.add).then_inc(s_mg, 1)

            def m_steps(j, first):
                hh, kv = HEADS, A_KV + B_HEADS
                c0 = j * 6 + CH_M
                for s in range(6):
                    split(c0 + (s + 1), CH_M + s + 1)
                    if s == 0:
                        if first:
                            k_split(kv - 1, 1)
                        else:
                            merge_b(j - 1)
                    if first and s == 1:
                        softmax(hh - 1, 1, None)
                        normalise(hh - 1, 1)
                    if first and s == 3:
                        o_split(hh - 1, 1)
                    if s == 3:
                        dve.wait_ge(s_sga, j + 1)
                        dve.wait_ge(s_chunk, c0 + 3)
                        V.tensor_tensor(t_a[:], sig_a[:], PS[:, 1, :], ALU.mult).then_inc(s_ta, 1)

            m_steps(0, True)
            with dve.Fori(1, KT) as j:
                own.loop(j, 1, 1)
                m_steps(j, False)
            own.done(KT - 1)

            def merged_split(j):
                dve.wait_ge(s_mhi, j + 1)
                V.tensor_tensor(m_lo[:, j, :], m_raw[:, j, :], m_hi[:, j, :].bitcast(F32), ALU.subtract).then_inc(s_mlo, 1)

            merged_split(0)
            merged_split(1)
            merge_b(KT - 1)

            def h_add(nn):
                dve.wait_ge(s_xres, 32 * (nn + 1))
                dve.wait_ge(s_chunk, CH_O + 8 * nn + 8)
                for t in range(NT):
                    hv = h[:, t, nn * S:nn * S + S]
                    V.tensor_tensor(hv, PS[:, t, :], x_part(t), ALU.add).then_inc(s_h, 1)

            def x_part(t):
                return x_res[:, t, :] if t < 3 else x_last[:]

            for nn in range(NT):
                for c in range(8):
                    n = CH_O + 8 * nn + c
                    if nn and c == 0:
                        h_add(nn - 1)
                    if n + 1 < CH_END:
                        split(n + 1, n + 1)
                    if nn == 0 and c < 7:
                        merged_split(2 * c + 2)
                        merged_split(2 * c + 3)
                    if nn == 0 and c == 7:
                        dve.wait_ge(s_wr, 32)
                        dve.wait_ge(s_wrg, 16 * 5)
                        V.tensor_tensor(wr[:], wr[:], bc(g2c[:], LOG), ALU.mult).then_inc(s_wrs, 1)
            h_add(NT - 1)
            routing(dve, own, V)
            dve.wait_ge(s_r1, 1)
            pairs = dve.value_load(nitem[0:1, 2:3], min_val=EXPERTS // 2, max_val=(EXPERTS + XTRA) // 2)
            g2b = bc(g2m[:], SLOTS)

            def x_copy(i):
                dve.wait_ge(s_xt2, i + 1)
                V.tensor_tensor(xT[:], PS[:, 2:4, :].rearrange("p a (k s) -> p (a k) s", s=SLOTS), g2b,
                                ALU.mult).then_inc(s_xTc, 1)

            def add_parts(p, parts):
                for r in parts:
                    t, m, bank = r // 2, r % 2, (2, 6)[r % 2]
                    dve.wait_ge(s_comb, p * 8 + (r + 1))
                    hv = h[:, t, :].rearrange("p (f m c) -> p m f c", f=2, m=2)[:, m]
                    V.tensor_tensor(hv, hv, PS[:, bank:bank + 2, :], ALU.add).then_inc(s_added, 1)

            dve.wait_ge(s_tok, 16)
            dve.wait_ge(s_r2, 1)
            for f in range(2):
                for y in (y_hi, y_lo):
                    V.tensor_scalar(y[f][:].rearrange("p (a b) -> p a b", a=2), rep(token[:], 2), 0.0, None, ALU.mult)
                last = V.tensor_scalar(place[f][:], token[:], 0.0, None, ALU.mult)
            last.then_inc(s_ylo, 1)
            dve.sem_inc(s_added, 2)
            dve.wait_ge(s_hd, 16 * NT)
            x_copy(0)
            with dve.Fori(0, pairs) as p:
                own.loop(p, 0, 4)
                for odd in range(2):
                    i = p * 2 + odd
                    if not odd:
                        add_parts(p, range(6))
                    dve.wait_ge(s_sgm, i + 1)
                    own.do(V.tensor_tensor(t1[:], sg[:], PS[:, 0, 0:F // 2], ALU.mult))
                    V.tensor_tensor(hs[:], t1[:], PS[:, 1, 0:F // 2], ALU.mult).then_inc(s_hs, 1)
                    if not odd:
                        add_parts(p, (6,))
                    dve.wait_ge(s_hst, i + 1)
                    V.tensor_copy(hT[:], PS[:, 0, 2 * P:4 * P].rearrange("p (c s) -> p c s", c=2)).then_inc(s_hTc, 1)
                    if not odd:
                        add_parts(p, (7,))
                    x_copy(i + 1)
                    own.do(V.tensor_copy(cur[:], tab[:, 0:2, ds(i, 1)].rearrange("p c o -> p (c o)")))
                    for f in range(2):
                        q = slice(SLOTS * (f ^ odd), SLOTS * (f ^ odd) + SLOTS)
                        V.tensor_scalar(place[f][q, :], token[q, :], cur[q, 0:1], None, ALU.is_equal)
                    dve.wait_ge(s_yhi, i + 1)
                    for f in range(2):
                        q = slice(SLOTS * (f ^ odd), SLOTS * (f ^ odd) + SLOTS)
                        last = V.scalar_tensor_tensor(out=y_lo[f][q, :], in0=PS[q, 4:6, :].rearrange("p a b -> p (a b)"),
                                                      scalar=cur[q, 1:2], in1=y_hi[f][q, :].bitcast(F32),
                                                      op0=ALU.mult, op1=ALU.subtract)
                    last.then_inc(s_ylo, 1)
            add_parts(pairs, range(8))

        @block.tensor
        def _(pe):
            mm = nc.tensor.matmul
            pe.wait_ge(s_const, 16)
            for G in range(16):
                t, kk = G // 4, G % 4
                if kk == 0:
                    pe.wait_ge(s_xn, t + 1)
                if G >= 8:
                    pe.wait_ge(s_xlo, G - 7)
                for q in range(4):
                    k = 4 * kk + q
                    last = nc.tensor.transpose(PS[:, G % 8, q * P:q * P + P], xt[:, t, k * P:k * P + P], ident)
                last.then_inc(s_xtr, 1)

            def chunk(n, python_n, bank, rhs_hi, rhs_lo, k0, start, stop, transposed=None):
                pe.wait_ge(s_wlo, n + 1)
                wh = w_hi[:, python_n % SPLIT, :].rearrange("p (k c) -> p k c", k=8)
                wl = w_lo[:, python_n % SPLIT, :].rearrange("p (k c) -> p k c", k=8)
                for k in range(8):
                    if k == 4 and transposed:
                        p_transpose(*transposed)
                    mm(PS[:, bank, :], wh[:, k, :], rhs_hi[:, k0 + k, :], start=(start and k == 0), stop=False)
                    mm(PS[:, bank, :], wh[:, k, :], rhs_lo[:, k0 + k, :], start=False, stop=False)
                    last = mm(PS[:, bank, :], wl[:, k, :], rhs_hi[:, k0 + k, :], start=False, stop=(stop and k == 7))
                last.then_inc(s_chunk, 1)

            def q_sums(hh, bank, kind):
                pe.wait_ge(s_sqq, hh + 1)
                for t in range(NT):
                    last = mm(PS[:, bank, t:t + 1], sq[:, t * P:t * P + P], ones[:, 0:1], start=True, stop=True)
                last.then_inc(s_qsum, 1)

            def k_sums(kv, bank):
                pe.wait_ge(s_sqk, kv + 1)
                mm(PS[:, bank, :], ones, sq[:], start=True, stop=True).then_inc(s_ksum, 1)

            def three(o, a_hi, a_lo, b_hi, b_lo, start=True, stop=True):
                mm(o, a_hi, b_hi, start=start, stop=False)
                mm(o, a_lo, b_hi, start=False, stop=False)
                return mm(o, a_hi, b_lo, start=False, stop=stop)

            def scores(hh, kind, kv):
                pe.wait_ge(s_qlo, hh + 1)
                pe.wait_ge(s_klo, kv + 1)
                for b in range(NT):
                    if kind == 0:
                        lo, hi = a_keys(b)
                        k0 = (b - 1) * P
                        qs = [q[:, b * P:b * P + P] for q in (q_hi, q_lo)]
                        ks = [k[:, k0 + lo:k0 + hi] for k in (k_hi, k_lo)]
                        o = PS[:, 2 + b, lo:hi]
                    else:
                        k0 = B_START[b] * ROWS
                        qs = [q[:, b * P:b * P + P] for q in (q_hi, q_lo)]
                        ks = [k[:, k0:k0 + 2 * P] for k in (k_hi, k_lo)]
                        o = PS[:, 2 + b // 2, (b % 2) * 256:(b % 2) * 256 + 256]
                    last = three(o, *qs, *ks)
                last.then_inc(s_sc, 1)

            def v_transpose(kv, kind):
                pe.wait_ge(s_vt, kv + 1)
                if kind == 0:
                    for t in range(NT):
                        last = nc.tensor.transpose(PS[:, 7, t * P:t * P + P], vt[:, t * P:t * P + P], ident)
                else:
                    for b in range(NT):
                        for kt in range(2):
                            c = (b % 2) * 256 + kt * P
                            last = nc.tensor.transpose(PS[:, 4 + b // 2, c:c + P],
                                                       vt[:, B_START[b] * ROWS + kt * P:B_START[b] * ROWS + kt * P + P],
                                                       ident)
                last.then_inc(s_vtr, 1)

            def p_transpose(hh, kind):
                for b in range(NT):
                    pe.wait_ge(s_p, hh * 4 + (b + 1))
                    lo, hi = a_keys(b) if kind == 0 else (0, 2 * P)
                    for c in range(lo, hi, P):
                        if kind == 0:
                            o = PS[:, 2 + b, c:c + P]
                        else:
                            o = PS[:, 4 + b // 2, (b % 2) * 256 + c:(b % 2) * 256 + c + P]
                        last = nc.tensor.transpose(o, prob[:, b, c:c + P], ident)
                last.then_inc(s_ptr, 1)

            def pv(hh, kind, kv):
                pe.wait_ge(s_ptc, hh + 1)
                pe.wait_ge(s_vtc, kv + 1)
                for b in range(NT):
                    lo, hi = a_keys(b) if kind == 0 else (0, 2 * P)
                    for c in range(lo, hi, P):
                        vi = (b - 1 + c // P) if kind == 0 else (2 * b + c // P)
                        last = mm(PS[:, 6, b * P:b * P + P], v_t[:, vi, :], p_t[:, b, c:c + P],
                                  start=(c == lo), stop=(c + P >= hi))
                last.then_inc(s_pv, 1)

            for g in range(A_KV):
                for s in range(12):
                    n, tile = 12 * g + s, s // 2
                    hh0 = A_GROUP * g
                    if s % 2 == 0:
                        if tile == 0 and g:
                            pe.wait_ge(s_qlo, hh0 - 1)
                            pe.wait_ge(s_sqq, hh0 - 1)
                        elif tile == 1 and g:
                            pe.wait_ge(s_qlo, hh0)
                            pe.wait_ge(s_sqq, hh0)
                        elif tile == 2:
                            pe.wait_ge(s_sqk, g + 1)
                        elif tile == 3:
                            pe.wait_ge(s_vt, g + 1)
                        elif tile > 3:
                            pe.wait_ge(s_qlo, hh0 + tile - 3)
                            pe.wait_ge(s_sqq, hh0 + tile - 3)
                    if n == 0:
                        pe.wait_ge(s_xlo, 16)
                    if s == 0:
                        transposed = (hh0 - 2, 0) if g else None
                    elif s == 2:
                        transposed = (hh0 - 1, 0) if g else None
                    else:
                        transposed = (hh0 + (s - 8) // 2, 0) if s >= 8 and s % 2 == 0 else None
                    chunk(n, n, tile % 2, x_hi, x_lo, 8 * (s % 2), s % 2 == 0, s % 2 == 1, transposed)
                    if n == 0:
                        pe.wait_ge(s_oh, 48)
                        mm(PS[0:A_HEADS, 7, :], small["table"][0:BUCKETS, :], onehot[:],
                           start=True, stop=True).then_inc(s_pos, 1)
                    if s == 0 and g:
                        pe.wait_ge(s_olo, hh0 - 2)
                        pv(hh0 - 2, 0, g - 1)
                        pe.wait_ge(s_rqs, hh0 - 1)
                        q_sums(hh0 - 1, 7, 0)
                        scores(hh0 - 1, 0, g - 1)
                    if s == 2:
                        if g:
                            pe.wait_ge(s_olo, hh0 - 1)
                            pv(hh0 - 1, 0, g - 1)
                            pe.wait_ge(s_rqs, hh0)
                        else:
                            pe.wait_ge(s_tv, 1)
                        k_sums(g, 7)
                    if s == 4:
                        pe.wait_ge(s_rks, g + 1)
                        v_transpose(g, 0)
                    if s >= 6 and s % 2 == 0:
                        hh = hh0 + (s - 6) // 2
                        if hh > hh0:
                            if hh > 1:
                                pe.wait_ge(s_olo, hh - 1)
                            pv(hh - 1, 0, g)
                            pe.wait_ge(s_rqs, hh)
                        else:
                            pe.wait_ge(s_vtc, g + 1)
                        q_sums(hh, 7, 0)
                        scores(hh, 0, g)

            def b_steps(h_, first):
                hh, kv, c0 = h_ + A_HEADS, h_ + A_KV, h_ * 6 + CH_B
                pk = 0 if first else 1
                for s in range(6):
                    if s == 0:
                        pe.wait_ge(s_qlo, hh - 1 if first else hh)
                        pe.wait_ge(s_sqq, hh - 1 if first else hh)
                    if s == 2:
                        pe.wait_ge(s_qlo, hh)
                        pe.wait_ge(s_sqq, hh)
                        pe.wait_ge(s_sqk, kv)
                    if s == 4:
                        if first:
                            pe.wait_ge(s_rqs, hh)
                        else:
                            pe.wait_ge(s_vt, kv)
                    if s == 0:
                        transposed = (A_HEADS - 2, 0) if first else None
                    elif s == 2:
                        if not first:
                            pe.wait_ge(s_vtc, kv)
                        transposed = (hh - 1, pk)
                    else:
                        transposed = None
                    chunk(c0 + s, CH_B + s, (0, 1, 7)[s // 2], x_hi, x_lo, 8 * (s % 2), s % 2 == 0, s % 2 == 1,
                          transposed)
                    if s == 0:
                        if first:
                            pe.wait_ge(s_olo, A_HEADS - 2)
                            pv(A_HEADS - 2, 0, A_KV - 1)
                            pe.wait_ge(s_rqs, A_HEADS - 1)
                            q_sums(A_HEADS - 1, 7, 0)
                            scores(A_HEADS - 1, 0, A_KV - 1)
                        else:
                            pe.wait_ge(s_rqs, hh)
                            v_transpose(kv - 1, 1)
                            scores(hh - 1, 1, kv - 1)
                    if s == 2:
                        pe.wait_ge(s_rks, kv)
                        pe.wait_ge(s_olo, hh - 1)
                        pv(hh - 1, pk, kv - 1)
                        q_sums(hh, 4, 1)
                    if s == 4:
                        pe.wait_ge(s_olo, hh)
                        k_sums(kv, 6)

            b_steps(0, True)
            with pe.Fori(1, B_HEADS) as h_:
                b_steps(h_, False)

            def m_steps(j, first):
                hh, kv, c0 = HEADS, A_KV + B_HEADS, j * 6 + CH_M
                for s in range(6):
                    if s == 0:
                        if first:
                            pe.wait_ge(s_sqq, hh)
                            pe.wait_ge(s_qlo, hh)
                        else:
                            pe.wait_ge(s_sga, j)
                    if s == 2:
                        if first:
                            pe.wait_ge(s_sqk, kv)
                        else:
                            pe.wait_ge(s_ta, j)
                    if s == 3:
                        if first:
                            pe.wait_ge(s_vt, kv)
                        else:
                            pe.wait_ge(s_sgb, j)
                    if s == 5:
                        if first:
                            pe.wait_ge(s_olo, hh)
                        else:
                            pe.wait_ge(s_mg, j)
                    n = c0 + s
                    pn = CH_M + s
                    if s < 2:
                        chunk(n, pn, 0, x_hi, x_lo, 8 * s, s == 0, s == 1)
                    elif s == 2:
                        if first:
                            pe.wait_ge(s_vtc, kv)
                        chunk(n, pn, 1, o_hi, o_lo, 0, True, True, (hh - 1, 1) if first else None)
                    elif s < 5:
                        chunk(n, pn, 7, x_hi, x_lo, 8 * (s - 3), s == 3, s == 4)
                    else:
                        chunk(n, pn, 6, o_hi, o_lo, A_HEADS, True, True)
                    if first and s == 0:
                        pe.wait_ge(s_rqs, hh)
                        v_transpose(kv - 1, 1)
                        scores(hh - 1, 1, kv - 1)
                    if first and s == 2:
                        pe.wait_ge(s_rks, kv)
                        pe.wait_ge(s_olo, hh - 1)
                        pv(hh - 1, 1, kv - 1)

            m_steps(0, True)
            with pe.Fori(1, KT) as j:
                m_steps(j, False)

            def h_transpose(k):
                pe.wait_ge(s_h, 4 * (k // 4) + 4)
                if k >= 2:
                    pe.wait_ge(s_htc, k - 1)
                for t in range(NT):
                    last = nc.tensor.transpose(PS[:, 4 + k % 2, t * P:t * P + P], h[:, t, k * P:k * P + P], ident)
                last.then_inc(s_htr, 1)

            def logits(k):
                pe.wait_ge(s_htc, k + 1)
                for t in range(NT):
                    last = mm(PS[:, 7, t * LOG:t * LOG + LOG], (h_t, h_t2)[k % 2][:, t * P:t * P + P], wr[:, k, :],
                              start=(k == 0 and t == 0), stop=(k == KT - 1 and t == NT - 1))
                last.then_inc(s_lg, 1)

            pe.wait_ge(s_sga, KT)
            pe.wait_ge(s_ta, KT)
            for nn in range(NT):
                for c in range(8):
                    n = CH_O + 8 * nn + c
                    pe.wait_ge(s_wlo, n + 1)
                    wh = w_hi[:, n % SPLIT, :].rearrange("p (k c) -> p k c", k=2)
                    wl = w_lo[:, n % SPLIT, :].rearrange("p (k c) -> p k c", k=2)
                    if nn == 0:
                        pe.wait_ge(s_mlo, 2 * c + 2)
                    for kk in range(2):
                        k = 2 * c + kk
                        for t in range(NT):
                            if k == 0 and nn:
                                pe.wait_ge(s_h, 4 * (nn - 1) + t + 1)
                            a, b = m_hi[:, k, t * P:t * P + P], m_lo[:, k, t * P:t * P + P]
                            last = three(PS[:, t, :], a, b, wh[:, kk, :], wl[:, kk, :], start=(k == 0), stop=(k == KT - 1))
                    last.then_inc(s_chunk, 1)
                    if nn and 1 <= c < 5:
                        h_transpose(4 * (nn - 1) + c - 1)
                    if nn and 2 <= c < 6:
                        if c == 2 and nn == 1:
                            pe.wait_ge(s_wrs, 1)
                        logits(4 * (nn - 1) + c - 2)
            k0 = 4 * NT - 4
            h_transpose(k0)
            for k in range(k0, 4 * NT):
                if k + 1 < 4 * NT:
                    h_transpose(k + 1)
                logits(k)
            pe.wait_ge(s_M, 3)
            mm(PS[:, 1, 0:160], ones, rt["before"][:].rearrange("p t e -> p (t e)"), start=True, stop=False)
            mm(PS[:, 1, 0:128], upper, rt["Ms"][:].rearrange("p t e -> p (t e)"), start=False, stop=True).then_inc(s_pos, 1)
            pe.wait_ge(s_ent, 1)
            for j in range(8):
                last = mm(PS[:, 0, 0:3 * ITEMS], rt["slot1h"][:, j, :], rt["entries"][:, j, :, :].rearrange("p c i -> p (c i)"),
                          start=(j == 0), stop=(j == 7))
            last.then_inc(s_tab, 1)
            pe.wait_ge(s_r1, 1)
            pairs = pe.value_load(nitem[0:1, 2:3], min_val=EXPERTS // 2, max_val=(EXPERTS + XTRA) // 2)
            pe.wait_ge(s_nreg, 1)

            def x_transpose(i):
                pe.wait_ge(s_xs, i + 1)
                settle(pe, s_pe_passed)
                v = xg[:].rearrange("s (p k) -> s k p", k=KT)
                for k in range(KT):
                    o = PS[:, 2 + k // 8, (k % 8) * SLOTS:(k % 8) * SLOTS + SLOTS]
                    last = nc.tensor.transpose(o, v[:, k, :], mats[0:SLOTS, 0, 0:SLOTS])
                last.then_inc(s_xt2, 1)

            def combine(p, c):
                for r in (2 * c, 2 * c + 1):
                    t, m, bank = r // 2, r % 2, (2, 6)[r % 2]
                    pe.wait_ge(s_added, p * 8 + (r + 1))
                    for y in (y_hi, y_lo):
                        for f in range(2):
                            last = mm(PS[:, bank + f, :], place[f][:, t * P:t * P + P], y[f][:, m * S:m * S + S],
                                      start=(y is y_hi), stop=(y is y_lo))
                    last.then_inc(s_comb, 1)

            x_transpose(0)

            def item(p, odd):
                i, gate = p * 2 + odd, (wg_s, wg_odd)[odd]
                pe.wait_ge(s_xTc, i + 1)
                for c in range(4):
                    pe.wait_ge(s_wg[odd][c], p * 16 + 16)
                    pe.wait_ge(s_wu[c], i * 16 + 16)
                    for k in range(4 * c, 4 * c + 4):
                        for bank, w in ((0, gate), (1, wu_s)):
                            for f in range(2):
                                last = mm(PS[SLOTS * f:SLOTS * f + SLOTS, bank, 0:F // 2], xT[:, k, :],
                                          w[:, k, f * (F // 2):(f + 1) * (F // 2)], start=(k == 0), stop=(k == KT - 1))
                    last.then_inc(s_gu, 1)
                    if not odd:
                        if c == 0:
                            pe.wait_ge(s_ylo, i + 1)
                        combine(p, c)
                if odd:
                    pe.wait_ge(s_added, p * 8 + 9)
                    x_transpose(i + 1)
                pe.wait_ge(s_hs, i + 1)
                hv = hs[:].rearrange("p (f c) -> p c f", c=2)
                for c in range(2):
                    last = nc.tensor.transpose(PS[:, 0, (2 + c) * P:(3 + c) * P], hv[:, c, :], ident)
                last.then_inc(s_hst, 1)
                if not odd:
                    pe.wait_ge(s_added, p * 8 + 9)
                    x_transpose(i + 1)
                pe.wait_ge(s_hTc, i + 1)
                pe.wait_ge(s_ylo, i + 1)
                for c in range(4):
                    j, cc = c // 2, c % 2
                    pe.wait_ge(s_wd[c], i * 16 + 16)
                    for m in range(2):
                        for f in range(2):
                            q = SLOTS * (f ^ odd)
                            last = mm(PS[q:q + SLOTS, 4 + m, :], hT[:, cc, SLOTS * j:SLOTS * j + SLOTS],
                                      wd_s[:, c, f * (D // 2) + m * S:f * (D // 2) + m * S + S],
                                      start=(c == 0), stop=(c == 3))
                    last.then_inc(s_dn, 1)

            with pe.Fori(0, pairs) as p:
                item(p, 0)
                item(p, 1)
            pe.wait_ge(s_ylo, pairs * 2 + 1)
            for c in range(NT):
                combine(pairs, c)


_INS = ['x', 'norm1_g', 'w_in', 'q_norm_a', 'k_norm_a', 'sink_a', 'q_norm_b', 'k_norm_b', 'rpb_b', 'w_up_a',
        'w_up_b', 'w_out', 'rel_bias_table', 'norm2_g', 'w_router_group', 'b_router_group',
        'w_router_expert', 'b_router_expert', 'w_gate', 'w_up', 'w_down']


def constants():
    f = np.float32
    i = np.arange(P)
    mats = np.stack([np.eye(P, dtype=f), np.ones((P, P), f), np.triu(np.ones((P, P), f), 1)], axis=1)
    rel = np.arange(S) - (2 * WINDOW - 1)
    half_b = BUCKETS // 2
    exact = half_b // 2
    n = np.abs(rel)
    nf = np.maximum(n, 1).astype(f)
    large = exact + (np.log(nf / f(exact)) / f(np.log(MAXDIST / exact)) * f(half_b - exact)).astype(np.int32)
    bucket = np.where(rel > 0, half_b, 0) + np.where(n < exact, n, np.minimum(large, half_b - 1))
    onehot = (bucket[None, :] == np.arange(BUCKETS)[:, None]).astype(f)
    mask_a = np.broadcast_to(np.where(n <= WINDOW, 0.0, NEG).astype(f), (A_HEADS, S))
    mask_b = np.zeros((P, 3, ROWS, KC), f)
    for b in range(NT):
        qc = QC * b + i // ROWS
        kc = B_START[b] + np.arange(KC)
        w0 = np.clip(qc - NB_COLS // 2, 0, GRID_W - NB_COLS)[:, None]
        ok = (kc[None, :] >= w0) & (kc[None, :] < w0 + NB_COLS)
        mask_b[:, B_KIND[b]] = np.where(ok, 0.0, NEG).astype(f)[:, None, :]
    ramp = np.zeros((P, 160 + SLOTS), f)
    ramp[:, 0:16] = np.tile([4, 3, 2, 1], 4)
    ramp[:, 32:160] = np.tile(np.arange(32, 0, -1), 4)
    ramp[:, 160:] = np.arange(SLOTS)
    entry = np.zeros((P, 3, 2, NT), f)
    entry[:, 0] = (i[:, None] + P * np.arange(NT)[None, :] - 2 * S)[:, None, :]
    tokens = np.broadcast_to(np.arange(S, dtype=f), (P, S))
    c = np.ascontiguousarray
    return {"c_mats": c(mats), "c_onehot": onehot, "c_maska": c(mask_a), "c_maskb": c(mask_b.reshape(P, 3, 2 * P)),
            "c_ramp": ramp, "c_entry": c(entry.reshape(P, 24)), "c_tokens": c(tokens)}


def kernel(**inputs):
    from concourse import bacc
    from concourse.bass_utils import run_bass_kernel_spmd as run

    nc = bacc.Bacc("TRN2", target_bir_lowering=False, num_devices=1)
    arrays, args = {}, []
    feed = [(n, np.ascontiguousarray(inputs[n])) for n in _INS]
    rpb = feed[8][1][0]
    pad = np.zeros((B_HEADS, 2 * NB_ROWS - 1, RPB_W), rpb.dtype)
    pad[:, :, NB_COLS:NB_COLS + 2 * NB_COLS - 1] = rpb
    feed[8] = ("rpb_pad", pad)
    feed += list(constants().items())
    for name, a in feed:
        arrays[f"in_{name}"] = a
        args.append(nc.dram_tensor(f"in_{name}", a.shape, mybir.dt.from_np(a.dtype), kind="ExternalInput").ap())
    for name, shape in (("tvec", [A_HEADS, S]), ("h", [S, D]), ("wide", [B_HEADS, P, ROWS * 3 * QC]), ("bias", [A_HEADS, P, 3 * P])):
        args.append(nc.dram_tensor(f"{name}_dram", shape, F32, kind="Internal").ap())
    args.append(nc.dram_tensor("out_0", [1, S, D], F32, kind="ExternalOutput").ap())
    build(nc, *args)
    r = run(nc, [arrays], core_ids=[0])
    return r.results[0]["out_0"]
```
